# Optimizing a Trainium2 kernel written in Bass

```python
import math
import jax, jax.numpy as jnp
from jax import lax
import numpy as np

D_MODEL = 1024
BATCH = 1
SEQ = 1024
DEPTH = 2
DEC_BATCH = 8
DEC_SEQ = 4
PAST_LEN = 4096
PAGE_SIZE = 128

N_EVEN = (DEPTH + 1) // 2
N_ODD = DEPTH // 2
CONV_CH_A = D_MODEL // 2
CONV_CH_B = D_MODEL // 2
IN_AB = 2 * CONV_CH_A + 3 * CONV_CH_B
KA = 31
KB = 3
KF = 3
HEAD_DIM = 64
N_HEADS = D_MODEL // HEAD_DIM
D_FF = ((8 * D_MODEL // 3 + 255) // 256) * 256
BRANCHES = ((128, 1), (512, 4), (2048, 16))
MAX_WINDOW = 2048
Q_BLOCK = 128
RMS_EPS = 1e-6
LN_EPS = 1e-5

kernel_name = "hybrid_conformerconv_shortconv_dilatedswa_convffn_step"

def rms_norm(x, g):
    xf = x.astype(jnp.float32)
    y = xf * lax.rsqrt(jnp.mean(xf * xf, axis=-1, keepdims=True) + RMS_EPS)
    return (y * g.astype(jnp.float32)).astype(x.dtype)

def causal_dwconv(x, state, w):
    k = w.shape[0]
    xp = jnp.concatenate([state.astype(x.dtype), x], axis=1)
    y = lax.conv_general_dilated(xp, w.astype(x.dtype)[:, None, :], (1,), 'VALID',
                                 dimension_numbers=('NWC', 'WIO', 'NWC'),
                                 feature_group_count=x.shape[-1])
    return y, xp[:, xp.shape[1] - (k - 1):]

def conv_mixers(h, st_a, st_b, w_in, wa, ba, lg, lb, wb, w_out):
    z = h @ w_in
    ca, cb = CONV_CH_A, CONV_CH_B
    glu = z[..., :ca] * jax.nn.sigmoid(z[..., ca:2 * ca])
    a, st_a_new = causal_dwconv(glu, st_a, wa)
    af = (a + ba.astype(a.dtype)).astype(jnp.float32)
    mu = jnp.mean(af, axis=-1, keepdims=True)
    var = jnp.mean(jnp.square(af - mu), axis=-1, keepdims=True)
    an = (af - mu) * lax.rsqrt(var + LN_EPS) * lg.astype(jnp.float32) + lb.astype(jnp.float32)
    a_out = (an * jax.nn.sigmoid(an)).astype(h.dtype)
    o = 2 * ca
    gate_b = z[..., o:o + cb]
    gate_c = z[..., o + cb:o + 2 * cb]
    x_t = z[..., o + 2 * cb:o + 3 * cb]
    cbo, st_b_new = causal_dwconv(gate_c * x_t, st_b, wb)
    b_out = gate_b * cbo
    y = jnp.concatenate([a_out, b_out], axis=-1) @ w_out
    return y, st_a_new, st_b_new

def conv_ffn(h, st, w_in, wc, w_down):
    z = h @ w_in
    g, st_new = causal_dwconv(z[..., :D_FF], st, wc)
    return (jax.nn.silu(g) * z[..., D_FF:]) @ w_down, st_new

def alibi_slopes():
    return jnp.asarray(2.0 ** (-8.0 * np.arange(1, N_HEADS + 1) / N_HEADS), dtype=jnp.float32)

def qkv_split(h, w_qkv):
    b, t, _ = h.shape
    z = (h @ w_qkv).reshape(b, t, 3, N_HEADS, HEAD_DIM)
    return z[:, :, 0], z[:, :, 1], z[:, :, 2]

def dilated_branch_prompt(q, k, v, steps, dil, slopes):
    bsz, s_len, nh, hd = q.shape
    sd = s_len // dil
    qb = math.gcd(sd, Q_BLOCK)
    nb = sd // qb
    qf = q.astype(jnp.float32).reshape(bsz, nb, qb, dil, nh, hd)
    pad = ((0, 0), (steps, 0), (0, 0), (0, 0), (0, 0))
    kp = jnp.pad(k.astype(jnp.float32).reshape(bsz, sd, dil, nh, hd), pad)
    vp = jnp.pad(v.astype(jnp.float32).reshape(bsz, sd, dil, nh, hd), pad)
    start = jnp.arange(nb) * qb
    idx = start[:, None] + jnp.arange(qb + steps)[None, :]
    kb = kp[:, idx]
    vb = vp[:, idx]
    s = jnp.einsum('bnirhc,bnjrhc->bnrhij', qf, kb) * (1.0 / math.sqrt(hd))
    ii = jnp.arange(qb)[:, None]
    jj = jnp.arange(qb + steps)[None, :]
    rel = ii + steps - jj
    valid = (rel >= 0) & (rel <= steps) & ((start[:, None, None] + jj - steps) >= 0)[:, :, :] 
    bias = -slopes[:, None, None] * (dil * rel).astype(jnp.float32)[None]
    s = jnp.where(valid[None, :, None, None], s + bias, -jnp.inf)
    m = jnp.max(s, axis=-1, keepdims=True)
    p = jnp.exp(s - m)
    l = jnp.sum(p, axis=-1)
    o = jnp.einsum('bnrhij,bnjrhc->bnirhc', p, vb)
    lt = jnp.transpose(l, (0, 1, 4, 2, 3))
    o = (o / lt[..., None]).reshape(bsz, s_len, nh, hd)
    lse = (jnp.transpose(m[..., 0], (0, 1, 4, 2, 3)) + jnp.log(lt)).reshape(bsz, s_len, nh)
    return o, lse

def dilated_branch_sample(q, kc, vc, buf_len, steps, dil, slopes):
    t = q.shape[1]
    hd = q.shape[-1]
    msteps = jnp.arange(steps + 1)
    idx = buf_len + jnp.arange(t)[:, None] - dil * msteps[None, :]
    valid = idx >= 0
    idxc = jnp.maximum(idx, 0)
    kg = kc.astype(jnp.float32)[:, idxc]
    vg = vc.astype(jnp.float32)[:, idxc]
    s = jnp.einsum('bthc,btmhc->bhtm', q.astype(jnp.float32), kg) * (1.0 / math.sqrt(hd))
    s = s - slopes[:, None, None] * (dil * msteps).astype(jnp.float32)[None, None, :]
    s = jnp.where(valid[None, None], s, -jnp.inf)
    m = jnp.max(s, axis=-1, keepdims=True)
    p = jnp.exp(s - m)
    l = jnp.sum(p, axis=-1)
    lt = jnp.transpose(l, (0, 2, 1))
    o = jnp.einsum('bhtm,btmhc->bthc', p, vg) / lt[..., None]
    lse = jnp.transpose(m[..., 0], (0, 2, 1)) + jnp.log(lt)
    return o, lse

def merge_branches(outs, lses):
    w = jax.nn.softmax(jnp.stack(lses, axis=0), axis=0)
    return jnp.sum(w[..., None] * jnp.stack(outs, axis=0), axis=0)

def dilated_attention_prompt(q, k, v, slopes):
    outs, lses = [], []
    for window, dil in BRANCHES:
        o, l = dilated_branch_prompt(q, k, v, window // dil, dil, slopes)
        outs.append(o)
        lses.append(l)
    return merge_branches(outs, lses)

def dilated_attention_sample(q, kc, vc, buf_len, slopes):
    outs, lses = [], []
    for window, dil in BRANCHES:
        o, l = dilated_branch_sample(q, kc, vc, buf_len, window // dil, dil, slopes)
        outs.append(o)
        lses.append(l)
    return merge_branches(outs, lses)

def setup_inputs(seed: int = 0) -> dict:
    key = jax.random.key(seed)
    ks = jax.random.split(key, 24)
    win_len = min(MAX_WINDOW, PAST_LEN)
    f32 = jnp.float32
    nrm = lambda k, shape, scale: jax.random.normal(k, shape, f32) * scale
    return {
        "x_prompt": nrm(ks[0], (BATCH, SEQ, D_MODEL), 1.0),
        "x_sample": nrm(ks[1], (DEC_BATCH, DEC_SEQ, D_MODEL), 1.0),
        "state_conv_a": nrm(ks[2], (N_EVEN, DEC_BATCH, KA - 1, CONV_CH_A), 0.5),
        "state_conv_b": nrm(ks[3], (N_EVEN, DEC_BATCH, KB - 1, CONV_CH_B), 1.0),
        "cache_k": nrm(ks[4], (N_ODD, DEC_BATCH, win_len, N_HEADS, HEAD_DIM), 1.0),
        "cache_v": nrm(ks[5], (N_ODD, DEC_BATCH, win_len, N_HEADS, HEAD_DIM), 1.0),
        "state_ffn": nrm(ks[6], (DEPTH, DEC_BATCH, KF - 1, D_FF), 1.0),
        "g_mix": 1.0 + nrm(ks[7], (DEPTH, D_MODEL), 0.02),
        "g_ffn": 1.0 + nrm(ks[8], (DEPTH, D_MODEL), 0.02),
        "g_final": 1.0 + nrm(ks[9], (D_MODEL,), 0.02),
        "w_in_ab": nrm(ks[10], (N_EVEN, D_MODEL, IN_AB), D_MODEL ** -0.5),
        "conv_a_w": nrm(ks[11], (N_EVEN, KA, CONV_CH_A), KA ** -0.5),
        "conv_a_b": nrm(ks[12], (N_EVEN, CONV_CH_A), 0.02),
        "ln_a_g": 1.0 + nrm(ks[13], (N_EVEN, CONV_CH_A), 0.02),
        "ln_a_b": nrm(ks[14], (N_EVEN, CONV_CH_A), 0.02),
        "conv_b_w": nrm(ks[15], (N_EVEN, KB, CONV_CH_B), KB ** -0.5),
        "w_out_ab": nrm(ks[16], (N_EVEN, CONV_CH_A + CONV_CH_B, D_MODEL), (CONV_CH_A + CONV_CH_B) ** -0.5),
        "w_qkv": nrm(ks[17], (N_ODD, D_MODEL, 3 * N_HEADS * HEAD_DIM), D_MODEL ** -0.5),
        "w_o": nrm(ks[18], (N_ODD, N_HEADS * HEAD_DIM, D_MODEL), (N_HEADS * HEAD_DIM) ** -0.5),
        "w_ffn_in": nrm(ks[19], (DEPTH, D_MODEL, 2 * D_FF), D_MODEL ** -0.5),
        "conv_f_w": nrm(ks[20], (DEPTH, KF, D_FF), KF ** -0.5),
        "w_down": nrm(ks[21], (DEPTH, D_FF, D_MODEL), D_FF ** -0.5),
    }

def reference(x_prompt, x_sample, state_conv_a, state_conv_b, cache_k, cache_v, state_ffn,
              g_mix, g_ffn, g_final, w_in_ab, conv_a_w, conv_a_b, ln_a_g, ln_a_b, conv_b_w, w_out_ab,
              w_qkv, w_o, w_ffn_in, conv_f_w, w_down):
    slopes = alibi_slopes()
    bp, bs = x_prompt.shape[0], x_sample.shape[0]
    buf_len = cache_k.shape[2]
    hp, hs = x_prompt, x_sample
    pa, sa, pb, sb, pk, sk, pv, sv, pf, sf = [], [], [], [], [], [], [], [], [], []
    for layer in range(DEPTH):
        i = layer // 2
        xn_p = rms_norm(hp, g_mix[layer])
        xn_s = rms_norm(hs, g_mix[layer])
        if layer % 2 == 0:
            za = jnp.zeros((bp, KA - 1, CONV_CH_A), hp.dtype)
            zb = jnp.zeros((bp, KB - 1, CONV_CH_B), hp.dtype)
            yp, na, nb_ = conv_mixers(xn_p, za, zb, w_in_ab[i], conv_a_w[i], conv_a_b[i],
                                      ln_a_g[i], ln_a_b[i], conv_b_w[i], w_out_ab[i])
            ys, ma, mb = conv_mixers(xn_s, state_conv_a[i], state_conv_b[i], w_in_ab[i], conv_a_w[i],
                                     conv_a_b[i], ln_a_g[i], ln_a_b[i], conv_b_w[i], w_out_ab[i])
            pa.append(na)
            pb.append(nb_)
            sa.append(ma)
            sb.append(mb)
        else:
            q, k, v = qkv_split(xn_p, w_qkv[i])
            att = dilated_attention_prompt(q, k, v, slopes)
            yp = att.reshape(bp, hp.shape[1], N_HEADS * HEAD_DIM).astype(hp.dtype) @ w_o[i]
            keep = min(MAX_WINDOW, k.shape[1])
            pk.append(k[:, k.shape[1] - keep:])
            pv.append(v[:, v.shape[1] - keep:])
            qs, ks_, vs_ = qkv_split(xn_s, w_qkv[i])
            kc = jnp.concatenate([cache_k[i].astype(ks_.dtype), ks_], axis=1)
            vc = jnp.concatenate([cache_v[i].astype(vs_.dtype), vs_], axis=1)
            att_s = dilated_attention_sample(qs, kc, vc, buf_len, slopes)
            ys = att_s.reshape(bs, hs.shape[1], N_HEADS * HEAD_DIM).astype(hs.dtype) @ w_o[i]
            sk.append(kc[:, kc.shape[1] - buf_len:])
            sv.append(vc[:, vc.shape[1] - buf_len:])
        hp = hp + yp
        hs = hs + ys
        zf = jnp.zeros((bp, KF - 1, D_FF), hp.dtype)
        fp, nfp = conv_ffn(rms_norm(hp, g_ffn[layer]), zf, w_ffn_in[layer], conv_f_w[layer], w_down[layer])
        fs, nfs = conv_ffn(rms_norm(hs, g_ffn[layer]), state_ffn[layer], w_ffn_in[layer], conv_f_w[layer], w_down[layer])
        hp = hp + fp
        hs = hs + fs
        pf.append(nfp)
        sf.append(nfs)
    y_prompt = rms_norm(hp, g_final)
    y_sample = rms_norm(hs, g_final)
    p_conv_a = jnp.stack(pa)
    s_conv_a = jnp.stack(sa)
    p_conv_b = jnp.stack(pb)
    s_conv_b = jnp.stack(sb)
    p_k = jnp.stack(pk)
    s_k = jnp.stack(sk)
    p_v = jnp.stack(pv)
    s_v = jnp.stack(sv)
    p_ffn = jnp.stack(pf)
    s_ffn = jnp.stack(sf)
    return (y_prompt, y_sample, p_conv_a, s_conv_a, p_conv_b, s_conv_b, p_k, s_k, p_v, s_v, p_ffn, s_ffn)


_drawn_inputs = setup_inputs


def setup_inputs(seed=0):
    import zlib

    import numpy as np

    out = dict(_drawn_inputs(seed))
    spreads = {}
    factors = {'g_final': 23.479, 'conv_a_b': 3.507, 'ln_a_g': 17.732, 'ln_a_b': 43.495, 'g_ffn': 2.796}
    for name, (base, spread) in spreads.items():
        noise = np.random.default_rng([zlib.crc32(name.encode()), seed]).standard_normal(out[name].shape)
        drawn = base * np.exp(spread * noise) if base else spread * noise
        out[name] = __import__('jax').numpy.asarray(drawn.astype(out[name].dtype))
    for name, factor in factors.items():
        out[name] = (out[name] * factor).astype(out[name].dtype)
    return out
```

```python
from contextlib import ExitStack

import numpy as np
import concourse.bass as bass
from concourse import mybir

F32 = mybir.dt.float32
F32R = mybir.dt.float32r
ALU = mybir.AluOpType
ACT = mybir.ActivationFunctionType
ds = bass.ds

P = 128
D = 1024
KD = D // P
NP_, NB, NQ = 1024, 8, 4
NS = NB * NQ
T = NP_ + NS
NT, TS = 3, T // 3
CA = 4
KA, KB, KF = 31, 3, 3
PAD = KA - 1
DFF = 2816
NJ = DFF // P
NG = NJ // 2
NH, HD = 16, 64
NPAIR = NH // 2
PAST = 2048
NKEY = 896
KT_TILES = NKEY // P
NKEYS = NKEY + NS
MASKED = -1.0e30
BRANCHES = ((128, 1), (512, 4), (2048, 16))
LN_EPS, RMS_EPS = 1e-5, 1e-6
KEPT = PAST - NQ

U_IN, U_OUT, U_FFN, U_QKV, U_WO = 0, 20, (28, 126), 94, 118
NUNITS = 192
MIX_ORDER = []
for _c in range(CA):
    MIX_ORDER += [("s", _c), ("a", _c)]
for _c in range(CA):
    MIX_ORDER += [("C", _c), ("X", _c), ("G", _c)]


def plan_uses():
    first, last, named, n = {}, {}, {}, 0

    def unit(u, k=1):
        nonlocal n
        first[u], last[u] = n, n + k - 1
        n += k

    def name(key, k=1):
        nonlocal n
        named[key] = n
        n += k

    name("stats0")
    unit(0)
    for u in range(1, 20):
        unit(u)
    name("ln_mean")
    name("ln_var")
    for u in range(20, 28):
        unit(u)
    for layer, key in ((0, "stats1"), (1, "stats3")):
        if layer == 1:
            name("stats2")
            for p in range(NPAIR):
                for x in range(3):
                    unit(U_QKV + 3 * p + x)
                name(("vrows", p))
                name(("scores", p), 16)
            for m in range(KD):
                unit(U_WO + m)
        u = U_FFN[layer]
        name(key)
        unit(u)
        for x in range(1, 4):
            unit(u + x)
        u += 4
        for _g in range(1, NG):
            for x in range(4):
                unit(u + x)
            for x in range(2):
                unit(u + 4 + x, 4)
            u += 6
        for x in range(2):
            unit(u + x, 4)
    name("stats4")
    return first, last, named


FIRST, LAST, NAMED = plan_uses()
SQ0 = {0: 0, "ln": 8, 1: 12, 2: 20, 3: 28, 4: 36}


def at(base, i, step):
    return base if i is None else i * step + base


def build(nc, xT, wstream, par, ident_d, ones_d, stA, stB, stF, kv, wtab, sbias, cache_k, cache_v,
          h_spill, o_y, o_pA, o_sA, o_pB, o_sB, o_kT, o_vT, o_sk, o_sv, o_pF, o_sF):
    base0 = (nc.sbuf_base + 31) // 32 * 32

    with ExitStack() as ctx:
        def place(name, shape, dt, off):
            size = int(np.prod(shape[1:])) * 4
            return nc.alloc_sbuf_tensor_at(name, shape, dt, offset=off), off + (size + 31) // 32 * 32

        def sem(name):
            return ctx.enter_context(nc.semaphore(name))

        off = base0
        H0 = off
        h, off = place("h", [P, KD, T], F32, off)
        X0 = off
        xs, off = place("xs", [P, 2, KD, T], F32R, off)
        M0 = off
        hid, off = place("hid", [P, 2, 2, 2, T], F32R, off)
        w_raw, off = place("w_raw", [P, 3, 1024], F32, off)
        w_sp, off = place("w_sp", [P, 3, 2, 1024], F32R, off)
        T0 = off
        rst, off = place("rst", [P, T], F32, off)
        ident, off = place("ident", [P, P], F32, off)
        ones, off = place("ones", [P, P], F32, off)
        NPAR = par.shape[1]
        pt, off = place("pt", [P, NPAR], F32, off)
        eps, off = place("eps", [P, 4], F32, off)
        T1 = off
        BS, off = place("BS", [P, CA, NB, KB - 1 + NQ], F32, off)
        pa_st, off = place("pa_st", [P, CA, PAD], F32, off)
        pb_st, off = place("pb_st", [P, CA, KB - 1], F32, off)
        sx, off = place("sx", [P, NJ, NB, KF - 1 + NQ], F32, off)
        pf_st, off = place("pf_st", [P, NJ, KF - 1], F32, off)
        g3, off = place("g3", [P, PAD + T], F32, off)
        spare, off = place("spare", [P, T], F32, off)
        AS, off = place("AS", [P, CA, NB, PAD + NQ], F32, off)
        tmp, off = place("tmp", [P, T], F32, off)
        sil, off = place("sil", [P, PAD + T], F32, off)
        acc, off = place("acc", [P, T], F32, off)
        assert off <= nc.sbuf_usable_end
        gbuf = g3
        g0, o2 = place("g0", [P, PAD + T], F32, M0)
        g1, o2 = place("g1", [P, PAD + T], F32, o2)
        g2, o2 = place("g2", [P, PAD + T], F32, o2)
        cb, o2 = place("cb", [P, CA, T], F32, o2)
        assert o2 <= M0 + 2 * 2 * 2 * T * 4
        G = [g0, g1, g2, g3]
        Y = [spare[:, :], g0[:, PAD:], g1[:, PAD:], g2[:, PAD:]]
        att, _ = place("att", [P, KD, T], F32, M0)
        neg_s, o2 = place("neg_s", [P, 2, 1024], F32, H0)
        wt, o2 = place("wt", [P, 2, 1024], F32, o2)
        kvr, o2 = place("kvr", [P, 4, NKEY], F32, o2)
        so, o2 = place("so", [P, 2, P], F32, o2)
        vnew, o2 = place("vnew", [NS, P], F32, o2)
        assert o2 <= X0
        QT, o2 = place("QT", [P, T], F32, T1)
        KT, o2 = place("KT", [P, T], F32, o2)
        VT, o2 = place("VT", [P, T], F32, o2)
        pT, o2 = place("pT", [P, 8, P], F32, o2)
        vrow, o2 = place("vrow", [P, 8, P], F32, o2)
        spT, o2 = place("spT", [P, 8, 88], F32, o2)
        qb, o2 = place("qb", [P, 8 * 72], F32, o2)
        qa, o2 = place("qa", [P, 64], F32, o2)
        sps, o2 = place("sps", [64, NKEYS], F32, o2)
        nmx, o2 = place("nmx", [P, 16], F32, o2)
        lsum, o2 = place("lsum", [P, 2, 16], F32, o2)
        snm, o2 = place("snm", [64, 8], F32, o2)
        assert o2 <= nc.sbuf_usable_end

        reg = [ctx.enter_context(nc.psum_tensor(f"reg{i}", [P, 3, 512], F32)) for i in range(2)]
        ob = ctx.enter_context(nc.psum_tensor("ob", [P, 2, 512], F32))

        def region(use):
            return reg[use % 2][:, :, 0:TS]

        def tok(ap):
            return ap.rearrange("p (s t) -> p s t", s=NT)

        cols, c0 = {}, 0
        for key, n in (("g", 5 * KD), ("wa", CA * KA), ("ba", CA), ("lg", CA), ("lb", CA), ("wb", CA * KB),
                       ("wf", 2 * NJ * KF)):
            cols[key] = c0
            c0 += n

        def pc(key, idx):
            return pt[:, cols[key] + idx:cols[key] + idx + 1]

        def pc_dyn(key, idx):
            return pt[:, ds(idx + cols[key], 1)] if not isinstance(idx, int) else pc(key, idx)

        par_in, st_in, sx_in = sem("par_in"), sem("st_in"), sem("sx_in")
        h_in = [sem(f"h_in{i}") for i in range(4)]
        w_in = [sem(f"w_in{i}") for i in range(3)]
        kv_in = [sem(f"kv_in{i}") for i in range(4)]
        wt_in = [sem(f"wt_in{i}") for i in range(2)]
        sb_in, h_back, kv_out = sem("sb_in"), sem("h_back"), sem("kv_out")
        copied, st_out, ff_out, y_out = sem("copied"), sem("st_out"), sem("ff_out"), sem("y_out")
        w_hi, w_lo = sem("w_hi"), sem("w_lo")
        full, free = sem("region_full"), sem("region_free")
        x_hi, x_lo = sem("x_hi"), sem("x_lo")
        sq_ok, sum_ok, std_ok = sem("sq_ok"), sem("sum_ok"), sem("std_ok")
        sig_ok, glu_ok, ysum_ok, ycen_ok, yn_ok = (sem(s) for s in ("sig_ok", "glu_ok", "ysum_ok", "ycen_ok", "yn_ok"))
        pads_ok = sem("pads_ok")
        conv_ok, silu_ok, silr_ok, hist_ok = (sem(s) for s in ("conv_ok", "silu_ok", "silr_ok", "hist_ok"))
        hid_hi, hid_lo = sem("hid_hi"), sem("hid_lo")
        y_ok = sem("y_ok")
        q_ok, ss_full, ss_free = sem("q_ok"), sem("ss_full"), sem("ss_free")
        kv_used, exp_ok, p_ok, pt_full, pt_a, pt_b, pv_ok, o_free = (
            sem(s) for s in ("kv_used", "exp_ok", "p_ok", "pt_full", "pt_a", "pt_b", "pv_ok", "o_free"))
        sp_exp, sp_ok, spt_full, spt_ok = (sem(s) for s in ("sp_exp", "sp_ok", "spt_full", "spt_ok"))
        so_ok, so_full, so_free = (sem(s) for s in ("so_ok", "so_full", "so_free"))
        v_chain, a_chain, g_chain = sem("v_chain"), sem("a_chain"), sem("g_chain")

        class Chain:

            def __init__(self, eng, s):
                self.eng, self.s, self.n = eng, s, 0

            def __call__(self, ins):
                ins.then_inc(self.s, 1)
                self.n += 1
                self.eng.wait_ge(self.s, self.n)

            def restart(self):
                self.eng.sem_clear(self.s)
                self.n = 0

        def in_unit(L, g, x):
            return U_FFN[L] + (x if g == 0 else 6 * g - 2 + x)

        def down_unit(L, g, x):
            return U_FFN[L] + (6 * (g + 1) + 2 + x if g < NG - 1 else 64 + x)

        class At:

            def __init__(self, i):
                self.i = i

            def unit(self, u):
                return at(u, self.i, 12)

            def use(self, r):
                return at(r, self.i, 24)

            def chunk(self, j):
                return at(j, self.i, 4)

        def load_unit(sp, u, slot, i=None, step=3):
            if i is not None or u >= 3:
                sp.wait_ge(w_lo, at(u - 2, i, step))
            src = wstream[u] if i is None else wstream[ds(i * step + u, 1), :, :].rearrange("a p c -> (a p) c")
            sp.dma_start(w_raw[:, slot, :], src).then_inc(w_in[slot], 16)

        def split_hi(act, u, i=None, step=12, used=None):
            act.wait_ge(w_in[u % 3], at(16 * (u // 3 + 1), i, 16 * step // 3))
            if used is not None:
                act.wait_ge(full, used)
            nc.scalar.activation(w_sp[:, u % 3, 0, :], w_raw[:, u % 3, :], ACT.Copy).then_inc(w_hi, 1)

        def split_lo(pool, u, i=None, step=12):
            pool.wait_ge(w_hi, at(u + 1, i, step))
            nc.gpsimd.tensor_tensor(w_sp[:, u % 3, 1, :], w_raw[:, u % 3, :], w_sp[:, u % 3, 0, :].bitcast(F32),
                                    ALU.subtract).then_inc(w_lo, 1)

        def hi_after(act, u, i=None, step=12, ustep=24):
            if u + 3 < NUNITS:
                split_hi(act, u + 3, i, step, at(LAST[u] + 1, i, ustep))

        def lo_after(pool, u, i=None, step=12):
            if u + 3 < NUNITS:
                split_lo(pool, u + 3, i, step)

        def h_ready(eng, s, m):
            if s == 0:
                eng.wait_ge(h_in[m // 2], 16)
            elif s == 1:
                eng.wait_ge(free, FIRST[U_OUT + m] + 1)
            elif s == 3:
                eng.wait_ge(free, FIRST[U_WO + m] + 1)
            else:
                L = 0 if s == 2 else 1
                eng.wait_ge(free, FIRST[down_unit(L, NG - 1, m // 4)] + m % 4 + 1)

        sqb = [sil[:, PAD:], tmp[:, :]]

        block = ctx.enter_context(nc.Block())

        @block.sync
        def _(sp):
            for dst, src in ((pt, par), (ident, ident_d), (ones, ones_d)):
                sp.dma_start(dst[:], src).then_inc(par_in, 16)
            for q in range(4):
                sp.dma_start(h[:, 2 * q:2 * q + 2, :], xT[:, 2 * q:2 * q + 2, :]).then_inc(h_in[q], 16)
                if q < 3:
                    load_unit(sp, q, q)
            for c in range(CA):
                sp.dma_start(AS[:, c, :, 0:PAD], stA[:, c]).then_inc(st_in, 16)
                sp.dma_start(BS[:, c, :, 0:KB - 1], stB[:, c]).then_inc(st_in, 16)
            for b in range(NB):
                sp.dma_start(sx[:, :, b, 0:KF - 1], stF[0, :, :, b]).then_inc(sx_in, 16)

            def copy_piece(b, x):
                cache, out = ((cache_k, o_sk), (cache_v, o_sv))[x // 2]
                half, n = x % 2, KEPT * D // 2
                if isinstance(b, int):
                    src, dst = cache[b], out[b]
                else:
                    src = cache[ds(b, 1), :].rearrange("a n -> (a n)")
                    dst = out[ds(b, 1), :].rearrange("a n -> (a n)")
                src = src[NQ * D + half * n:NQ * D + (half + 1) * n].rearrange("(e r c) -> e r c", e=16, c=896)
                dst = dst[half * n:(half + 1) * n].rearrange("(e r c) -> e r c", e=16, c=896)
                sp.dma_start(dst, src).then_inc(copied, 16)

            with sp.Fori(0, NB - 1) as i:
                for x in range(4):
                    for s in range(3):
                        load_unit(sp, 3 + 3 * x + s, s, i, 12)
                    copy_piece(i, x)
            for x in range(4):
                for s in range(3):
                    if 87 + 3 * x + s <= 94:
                        load_unit(sp, 87 + 3 * x + s, s)
                copy_piece(NB - 1, x)
            sp.wait_ge(ysum_ok, 1)
            sp.dma_start(o_pA, pa_st[:]).then_inc(st_out, 16)
            sp.dma_start(o_pB, pb_st[:]).then_inc(st_out, 16)
            for c in range(CA):
                sp.dma_start(o_sA[:, c], AS[:, c, :, NQ:]).then_inc(st_out, 16)
                sp.dma_start(o_sB[:, c], BS[:, c, :, NQ:]).then_inc(st_out, 16)

            def store_ffn_state(L):
                sp.wait_ge(hist_ok, 2 * NJ * (L + 1))
                sp.dma_start(o_pF[L], pf_st[:]).then_inc(ff_out, 16)
                for b in range(NB):
                    sp.dma_start(o_sF[L, :, :, b], sx[:, :, b, NQ:]).then_inc(ff_out, 16)

            store_ffn_state(0)
            load_unit(sp, 95, 2)
            load_unit(sp, 96, 0)
            for m in range(KD):
                h_ready(sp, 2, m)
            sp.dma_start(h_spill, h[:]).then_inc(kv_out, 16)
            sp.wait_ge(kv_out, 16)
            sp.wait_ge(x_lo, 8 * 4)
            sp.wait_ge(x_hi, 8 * 4)
            sp.wait_ge(sum_ok, SQ0[2] + KD)
            sp.wait_ge(ff_out, 16 * (1 + NB))
            sp.wait_ge(st_out, 16 * (2 + 2 * CA))
            sp.wait_ge(free, NAMED["stats2"] + 1)
            for hh in range(2):
                sp.dma_start(wt[:, hh, :], wtab[hh]).then_inc(wt_in[hh], 16)
            sp.dma_start(sps[:], sbias[0]).then_inc(sb_in, 16)

            def kv_item(p, x):
                src = kv[ds(p, 1), x].rearrange("a p c -> (a p) c")
                sp.dma_start(kvr[:, x % 4, :], src).then_inc(kv_in[x % 4], 16)

            r0 = FIRST[U_QKV]
            with sp.Fori(0, NPAIR) as p:
                sp.wait_ge(so_free, p + 1)
                for x in range(16):
                    if x == 4:
                        for y in range(3):
                            load_unit(sp, 97 + y, (97 + y) % 3, p, 3)
                        sp.wait_ge(free, p * 20 + (r0 + 2))
                        sp.dma_start(o_kT[ds(p, 1)].rearrange("a p c -> (a p) c"), KT[:]).then_inc(kv_out, 16)
                        sp.wait_ge(free, p * 20 + (r0 + 3))
                        sp.dma_start(o_vT[ds(p, 1)].rearrange("a p c -> (a p) c"), VT[:]).then_inc(kv_out, 16)
                    if x >= 4:
                        sp.wait_ge(kv_used, p * 16 + (x - 3))
                    kv_item(p, x)
                sp.wait_ge(free, p * 20 + (r0 + 4 + 8))
                sp.dma_start(wt[:, 0, :], wtab[ds(p * 2 + 2, 1)].rearrange("a p c -> (a p) c")).then_inc(wt_in[0], 16)
                sp.wait_ge(free, p * 20 + (r0 + 4 + 16))
                sp.dma_start(wt[:, 1, :], wtab[ds(p * 2 + 3, 1)].rearrange("a p c -> (a p) c")).then_inc(wt_in[1], 16)
                sp.wait_ge(spt_full, p + 1)
                sp.dma_start(sps[:], sbias[ds(p + 1, 1)].rearrange("a p c -> (a p) c")).then_inc(sb_in, 16)
            sp.wait_ge(so_free, NPAIR + 1)
            sp.wait_ge(o_free, 1 + 4 * NPAIR)
            sp.wait_ge(free, r0 + 20 * NPAIR)
            sp.wait_ge(wt_in[0], 16 * (NPAIR + 1))
            sp.wait_ge(wt_in[1], 16 * (NPAIR + 1))
            sp.wait_ge(sb_in, 16 * (NPAIR + 1))
            sp.wait_ge(kv_out, 16 + 32 * NPAIR)
            sp.dma_start(h[:], h_spill).then_inc(h_back, 16)
            for b in range(NB):
                sp.dma_start(sx[:, :, b, 0:KF - 1], stF[1, :, :, b]).then_inc(sx_in, 16)
            n_left = NUNITS + 1 - 121
            with sp.Fori(0, n_left // 3) as i:
                for s in range(3):
                    load_unit(sp, 121 + s, (121 + s) % 3, i, 3)
            for s in range(n_left % 3):
                load_unit(sp, 121 + n_left // 3 * 3 + s, (121 + n_left // 3 * 3 + s) % 3)
            store_ffn_state(1)
            for m in range(KD):
                sp.wait_ge(y_ok, m + 1)
                sp.dma_start(o_y[:, m], h[:, m, :]).then_inc(y_out, 16)
            sp.wait_ge(copied, 16 * 4 * NB)
            sp.wait_ge(st_out, 16 * (2 + 2 * CA))
            sp.wait_ge(ff_out, 2 * 16 * (1 + NB))
            sp.wait_ge(y_out, 16 * KD)

        @block.tensor
        def _(pe):
            def open_use(r, i=None, step=24):
                if i is not None or r >= 2:
                    pe.wait_ge(free, at(r - 1, i, step))

            def in_proj(u, r, i=None, ustep=12, rstep=24, x_at=None, order=range(KD)):
                pe.wait_ge(w_lo, at(u + 1, i, ustep))
                open_use(r, i, rstep)
                out = region(r)
                w = w_sp[:, u % 3]
                for n, k in enumerate(order):
                    if x_at is not None:
                        pe.wait_ge(x_lo, x_at + n + 1)
                    for wh, xh in ((0, 0), (0, 1), (1, 0)):
                        for t in range(NT):
                            mm = nc.tensor.matmul(out[:, t, :], w[:, wh, k * P:(k + 1) * P],
                                                  xs[:, xh, k, t * TS:(t + 1) * TS],
                                                  start=(n == 0 and wh + xh == 0), stop=(n == KD - 1 and wh == 1))
                mm.then_inc(full, 1)

            def down_proj(u, r, par_g, i=None):
                pe.wait_ge(w_lo, at(u + 1, i, 12))
                w = w_sp[:, u % 3]
                for m in range(4):
                    open_use(r + m, i)
                    out = region(r + m)
                    for kk in range(2):
                        for wh, xh in ((0, 0), (0, 1), (1, 0)):
                            for t in range(NT):
                                mm = nc.tensor.matmul(out[:, t, :], w[:, wh, kk * 512 + m * P:kk * 512 + (m + 1) * P],
                                                      hid[:, par_g, kk, xh, t * TS:(t + 1) * TS],
                                                      start=(kk == 0 and wh + xh == 0), stop=(kk == 1 and wh == 1))
                    mm.then_inc(full, 1)

            def column_means(r, ready, src):
                pe.wait_ge(*ready)
                open_use(r)
                for t in range(NT):
                    mm = nc.tensor.matmul(region(r)[:, t, :], ones[:, :], src[:, t * TS:(t + 1) * TS],
                                          start=True, stop=True)
                mm.then_inc(full, 1)

            pe.wait_ge(par_in, 48)
            in_proj(0, FIRST[0], x_at=0)
            column_means(NAMED["stats0"], (sum_ok, KD), acc)
            in_proj(1, FIRST[1])
            with pe.Fori(0, 3) as i:
                for x in range(6):
                    in_proj(2 + x, FIRST[2 + x], i, 6, 6)
            column_means(NAMED["ln_mean"], (ysum_ok, 1), acc)
            column_means(NAMED["ln_var"], (sum_ok, SQ0["ln"] + CA), acc)
            for m in range(KD):
                in_proj(U_OUT + m, FIRST[U_OUT + m], x_at=KD if m == 0 else None, order=(4, 5, 6, 7, 0, 1, 2, 3))

            def ffn(L):
                s, e = (1, 2) if L == 0 else (3, 5)
                in_proj(in_unit(L, 0, 0), FIRST[in_unit(L, 0, 0)], x_at=e * KD)
                column_means(NAMED[f"stats{s}"], (sum_ok, SQ0[s] + KD), acc)
                for x in range(1, 4):
                    in_proj(in_unit(L, 0, x), FIRST[in_unit(L, 0, x)])

                def down(g, i):
                    pe.wait_ge(hid_lo, at(NJ * L + 2 * g + 2, i, 4))
                    for x in range(2):
                        u = down_unit(L, g, x)
                        down_proj(u, FIRST[u], g % 2, i)

                with pe.Fori(0, (NG - 1) // 2) as i:
                    for g in (1, 2):
                        for x in range(4):
                            u = in_unit(L, g, x)
                            in_proj(u, FIRST[u], i)
                        down(g - 1, i)
                down(NG - 1, None)

            ffn(0)

            column_means(NAMED["stats2"], (sum_ok, SQ0[2] + KD), acc)
            pe.wait_ge(x_lo, 4 * KD)
            r0 = FIRST[U_QKV]
            pe.wait_ge(o_free, 1)
            with pe.Fori(0, NPAIR) as p:
                def opened(r):
                    pe.wait_ge(free, p * 20 + (r - 1))

                for x in range(3):
                    in_proj(U_QKV + x, r0 + x, p, 3, 20)

                pe.wait_ge(q_ok, p + 1)
                pe.wait_ge(o_free, p * 4 + 1)
                for b in range(NB):
                    pe.wait_ge(kv_in[b % 4], p * 64 + 16 * (b // 4 + 1))
                    for bank, lo, hi_ in ((0, 0, 512), (1, 512, NKEY)):
                        mm = nc.tensor.matmul(ob[0:64, bank, 0:hi_ - lo], qb[:, 64 * b:64 * b + 64],
                                              kvr[:, b % 4, lo:hi_], start=(b == 0), stop=(b == NB - 1))
                    mm.then_inc(kv_used, 1)
                pe.wait_ge(free, p * 20 + (r0 + 2))
                nc.tensor.matmul(ob[0:64, 1, NKEY - 512:NKEYS - 512], qa[:, :], KT[:, NP_:T],
                                 start=True, stop=True).then_inc(ss_full, 1)

                pe.wait_ge(free, p * 20 + (r0 + 3))
                vr = reg[(r0 + 3) % 2]
                for t in range(8):
                    nc.tensor.transpose(vr[:, t // 4, (t % 4) * P:(t % 4 + 1) * P], VT[:, t * P:(t + 1) * P], ident[:, :])
                nc.tensor.transpose(vr[0:NS, 2, 0:P], VT[:, NP_:T], ident[:, :]).then_inc(full, 1)

                def scores(n):
                    hh, b = n // 8, n % 8
                    opened(r0 + 4 + n)
                    out = reg[(r0 + 4 + n) % 2]
                    for lo in range(0, P * (b + 1), 512):
                        w = min(512, P * (b + 1) - lo)
                        mm = nc.tensor.matmul(out[:, lo // 512, 0:w], QT[HD * hh:HD * hh + HD, b * P:(b + 1) * P],
                                              KT[HD * hh:HD * hh + HD, lo:lo + w], start=True, stop=True)
                    mm.then_inc(full, 1)

                def turn(n):
                    b = n % 8
                    pe.wait_ge(p_ok, p * 16 + (n + 1))
                    for kb in range(b + 1):
                        mm = nc.tensor.transpose(reg[kb // 4][:, 2, (kb % 4) * P:(kb % 4 + 1) * P],
                                                 neg_s[:, n % 2, kb * P:(kb + 1) * P], ident[:, :])
                    mm.then_inc(pt_full, 1)

                def weigh(n):
                    hh, b = n // 8, n % 8
                    pe.wait_ge(pt_a, p * 16 + (n + 1))
                    if b >= 4:
                        pe.wait_ge(pt_b, p * 8 + (4 * hh + b - 3))
                    if n == 0:
                        pe.wait_ge(ss_free, p + 1)
                        pe.wait_ge(free, p * 20 + (r0 + 4))
                    if n == 4:
                        pe.wait_ge(spt_ok, p * 2 + 2)
                    if n in (8, 12):
                        pe.wait_ge(o_free, p * 4 + (2 + (n - 8) // 4))
                    for kb in range(b + 1):
                        mm = nc.tensor.matmul(ob[:, b // 4, (b % 4) * P:(b % 4 + 1) * P],
                                              vrow[:, kb, :], pT[:, kb, :],
                                              start=(kb == 0), stop=(kb == b))
                    mm.then_inc(pv_ok, 1)

                def turn_sample():
                    pe.wait_ge(sp_ok, p + 1)
                    for t in range(KT_TILES):
                        nc.tensor.matmul(ob[:, 1, 64 * t:64 * t + 64], sps[:, t * P:(t + 1) * P], ident[0:64, 0:64],
                                         start=True, stop=True)
                    nc.tensor.matmul(ob[0:NS, 1, 448:512], sps[:, NKEY:NKEYS], ident[0:64, 0:64],
                                     start=True, stop=True).then_inc(spt_full, 1)

                def weigh_sample(b):
                    pe.wait_ge(kv_in[b % 4], p * 64 + 16 * (2 + b // 4 + 1))
                    out = reg[1][32 * (b % 4):32 * (b % 4) + 32, 2, P * (b // 4):P * (b // 4) + P]
                    for t in range(KT_TILES):
                        nc.tensor.matmul(out, spT[:, t, 8 * b:8 * b + 32], kvr[:, b % 4, t * P:(t + 1) * P],
                                         start=(t == 0), stop=False)
                    nc.tensor.matmul(out, spT[0:NS, 7, 8 * b:8 * b + 32], vnew[:, :],
                                     start=False, stop=True).then_inc(kv_used, 1)

                scores(0)
                scores(1)
                for n in range(16):
                    if n == 12:
                        pe.wait_ge(so_free, p + 2)
                    turn(n)
                    if n + 2 < 16:
                        scores(n + 2)
                    if n in (8, 9, 10):
                        for b in ((0, 1, 2), (3, 4, 5), (6, 7))[n - 8]:
                            weigh_sample(b)
                    weigh(n)
                    if n == 0:
                        turn_sample()
                    if n == 11:
                        pe.wait_ge(so_ok, p + 1)
                        for x in range(2):
                            mm = nc.tensor.transpose(reg[1][:, 2, 256 + P * x:256 + P * x + P], so[:, x, :], ident[:, :])
                        mm.then_inc(so_full, 1)

            for m in range(KD):
                in_proj(U_WO + m, FIRST[U_WO + m], x_at=4 * KD if m == 0 else None)
            ffn(1)
            column_means(NAMED["stats4"], (sum_ok, SQ0[4] + KD), acc)

        @block.scalar
        def _(act):
            chain = Chain(act, a_chain)

            def square(s, m, src):
                k = SQ0[s] + m
                if k >= 2:
                    act.wait_ge(sum_ok, k - 1)
                nc.scalar.activation(sqb[k % 2], src, ACT.Square).then_inc(sq_ok, 1)

            def gain_hi(s, e, m):
                nc.scalar.activation(xs[:, 0, m, :], h[:, m, :], ACT.Copy, scale=pc("g", s * KD + m)).then_inc(x_hi, 1)

            def std(r, dst, scale, e, late=False):
                act.wait_ge(full, r + (2 if late else 1))
                nc.scalar.activation(tok(dst), region(r), ACT.Sqrt, bias=eps[:, e:e + 1], scale=scale).then_inc(std_ok, 1)

            act.wait_ge(par_in, 48)
            act.wait_ge(pads_ok, 1)
            for u in range(3):
                split_hi(act, u)
            for m in range(KD):
                h_ready(act, 0, m)
                gain_hi(0, 0, m)
                square(0, m, h[:, m, :])
            hi_after(act, 0)
            std(NAMED["stats0"], rst[:, :], 1.0, 0, late=True)
            for c in range(CA):
                if c > 0:
                    hi_after(act, 2 * c)
                act.wait_ge(free, FIRST[2 * c] + 1)
                if c > 0:
                    act.wait_ge(glu_ok, c)
                nc.scalar.activation(sil[:, PAD:], tmp[:, :], ACT.Sigmoid).then_inc(sig_ok, 1)
                hi_after(act, 2 * c + 1)
            for u in range(8, 20):
                hi_after(act, u)
            for c in range(CA):
                if c < CA - 1:
                    act.wait_ge(ycen_ok, c + 1)
                else:
                    act.wait_ge(free, NAMED["ln_mean"] + 1)
                square("ln", c, Y[c])
            std(NAMED["ln_var"], tmp[:, :], 2.0, 1)
            act.wait_ge(full, LAST[19] + 1)
            for c in range(CA):
                act.wait_ge(free, FIRST[10 + 3 * c] + 1)
                nc.scalar.activation(xs[:, 0, CA + c, :], cb[:, c, :], ACT.Copy).then_inc(x_hi, 1)
            for c in range(CA):
                act.wait_ge(yn_ok, c + 1)
                chain(nc.scalar.activation(Y[c], Y[c], ACT.Silu, scale=pc("lg", c), bias=pc("lb", c)))
                nc.scalar.activation(xs[:, 0, c, :], Y[c], ACT.Copy).then_inc(x_hi, 1)
            for m in range(KD):
                hi_after(act, U_OUT + m)
                h_ready(act, 1, m)
                square(1, m, h[:, m, :])

            def ffn(L):
                s, e = (1, 2) if L == 0 else (3, 5)
                act.wait_ge(full, LAST[(U_OUT, U_WO)[L] + KD - 1] + 1)
                for m in range(KD):
                    h_ready(act, s, m)
                    gain_hi(s, e, m)
                hi_after(act, in_unit(L, 0, 0))
                std(NAMED[f"stats{s}"], rst[:, :], 1.0, 0, late=True)

                def chunk(g, c, i, skip=False):
                    A = At(i)
                    j = NJ * L + 2 * g + c
                    ug, uu = in_unit(L, g, 2 * c), in_unit(L, g, 2 * c + 1)
                    if not skip:
                        hi_after(act, ug, i)
                    act.wait_ge(conv_ok, A.chunk(j + 1))
                    nc.scalar.activation(sil[:, PAD:], acc[:, :], ACT.Silu).then_inc(silu_ok, 1)
                    hi_after(act, uu, i)
                    act.wait_ge(free, A.use(FIRST[uu] + 1))
                    nc.scalar.activation(hid[:, g % 2, c, 0, :], tmp[:, :], ACT.Copy).then_inc(hid_hi, 1)

                chunk(0, 0, None, skip=True)
                chunk(0, 1, None)
                with act.Fori(0, (NG - 1) // 2) as i:
                    for g in (1, 2):
                        for c in range(2):
                            chunk(g, c, i)
                        for x in range(2):
                            hi_after(act, down_unit(L, g - 1, x), i)
                s2 = 2 if L == 0 else 4
                for m in range(KD):
                    h_ready(act, s2, m)
                    if m == 0:
                        act.wait_ge(hid_lo, NJ * (L + 1))
                    if L == 0:
                        gain_hi(2, 3, m)
                    square(s2, m, h[:, m, :])
                    if m % 4 == 3:
                        hi_after(act, down_unit(L, NG - 1, m // 4))

            ffn(0)
            std(NAMED["stats2"], rst[:, :], 1.0, 0)
            r0 = FIRST[U_QKV]
            with act.Fori(0, NPAIR) as p:
                act.wait_ge(ss_free, p + 1)
                nc.scalar.activation(sps[:, :], sps[:, :], ACT.Exp, bias=snm[:, 0:1], scale=-1.0,
                                     accum_out=snm[:, 1:2]).then_inc(sp_exp, 1)

                def probs(n):
                    b = n % 8
                    act.wait_ge(free, p * 20 + (r0 + 5 + n))
                    nc.scalar.activation(neg_s[:, n % 2, 0:P * (b + 1)], neg_s[:, n % 2, 0:P * (b + 1)], ACT.Exp,
                                         bias=nmx[:, n:n + 1], scale=-1.0,
                                         accum_out=lsum[:, 0, n:n + 1]).then_inc(exp_ok, 1)

                def outputs(hh, half):
                    act.wait_ge(pv_ok, p * 16 + (8 * hh + 4 * half + 4))
                    rows = slice(HD * hh, HD * hh + HD)
                    dst = att[rows, ds(p, 1), 512 * half:512 * half + 512].rearrange("p a t -> p (a t)")
                    nc.scalar.activation(dst, ob[rows, half, :], ACT.Copy).then_inc(o_free, 1)

                probs(0)
                probs(1)
                for x in range(3):
                    split_hi(act, U_QKV + 3 + x, p, 3, p * 20 + (r0 + x + 1))
                for n in range(16):
                    b = n % 8
                    if b >= 4:
                        act.wait_ge(pt_full, p * 16 + (n + 1))
                        nc.scalar.activation(pT[:, 4:b + 1, :], reg[1][:, 2, 0:P * (b - 3)].rearrange("p (k q) -> p k q", q=P),
                                             ACT.Copy).then_inc(pt_b, 1)
                    if n + 2 < 16:
                        probs(n + 2)
                    if n == 0:
                        act.wait_ge(spt_full, p + 1)
                        nc.scalar.activation(spT[:, 0:7, 0:64], ob[:, 1, 0:448].rearrange("p (t r) -> p t r", r=64),
                                             ACT.Copy).then_inc(spt_ok, 1)
                        nc.scalar.activation(spT[0:NS, 7, 0:64], ob[0:NS, 1, 448:512], ACT.Copy).then_inc(spt_ok, 1)
                    if n == 10:
                        act.wait_ge(kv_used, p * 16 + 16)
                        nc.scalar.activation(so[:, :, :], reg[1][:, 2, 0:256].rearrange("p (x c) -> p x c", c=P),
                                             ACT.Copy).then_inc(so_ok, 1)
                    if n in (5, 9, 13):
                        outputs((n - 5) // 4 // 2, (n - 5) // 4 % 2)
                outputs(1, 1)
            act.wait_ge(so_free, NPAIR + 1)
            act.wait_ge(o_free, 1 + 4 * NPAIR)
            for m in range(KD):
                nc.scalar.activation(xs[:, 0, m, :], att[:, m, :], ACT.Copy).then_inc(x_hi, 1)
            for m in range(KD):
                hi_after(act, U_WO + m)
                h_ready(act, 3, m)
                square(3, m, h[:, m, :])
            ffn(1)
            std(NAMED["stats4"], rst[:, :], 1.0, 0)

        @block.gpsimd
        def _(pool):
            def add_square(s, m):
                k = SQ0[s] + m
                pool.wait_ge(sq_ok, k + 1)
                if m == 0:
                    if s == "ln":
                        pool.wait_ge(ycen_ok, 1)
                    nc.gpsimd.tensor_copy(acc[:, :], sqb[k % 2]).then_inc(sum_ok, 1)
                else:
                    pool.wait_ge(sum_ok, k)
                    nc.gpsimd.tensor_tensor(acc[:, :], acc[:, :], sqb[k % 2], ALU.add).then_inc(sum_ok, 1)

            for u in range(3):
                split_lo(pool, u)
            for m in range(KD):
                add_square(0, m)
            for u in range(20):
                lo_after(pool, u)
            for c in range(CA):
                add_square("ln", c)
            for m in range(KD):
                lo_after(pool, U_OUT + m)
                add_square(1, m)

            def ffn(L):
                def chunk(g, c, i):
                    A = At(i)
                    jj = 2 * g + c
                    j = NJ * L + jj
                    ug, uu = in_unit(L, g, 2 * c), in_unit(L, g, 2 * c + 1)
                    lo_after(pool, ug, i)
                    pool.wait_ge(free, A.use(FIRST[ug] + 1))
                    if g == 0 and c == 0:
                        pool.wait_ge(sx_in, 16 * NB * (L + 1))
                        if L == 1:
                            pool.wait_ge(ff_out, 16 * (1 + NB))
                    if i is None:
                        sx_j, pf_j = sx[:, jj, :, KF - 1:], pf_st[:, jj, :]
                    else:
                        sx_j = sx[:, ds(i * 4 + jj, 1), :, KF - 1:].rearrange("p a b q -> p (a b) q")
                        pf_j = pf_st[:, ds(i * 4 + jj, 1), :].rearrange("p a k -> p (a k)")
                    nc.gpsimd.tensor_copy(sx_j, gbuf[:, PAD + NP_:].rearrange("p (b q) -> p b q", b=NB)).then_inc(hist_ok, 1)
                    nc.gpsimd.tensor_copy(pf_j, gbuf[:, PAD + NP_ - KF + 1:PAD + NP_]).then_inc(hist_ok, 1)
                    lo_after(pool, uu, i)
                    pool.wait_ge(silu_ok, A.chunk(j + 1))
                    nc.gpsimd.tensor_tensor(sil[:, PAD:], sil[:, PAD:], rst[:, :], ALU.mult).then_inc(silr_ok, 1)

                for c in range(2):
                    chunk(0, c, None)
                with pool.Fori(0, (NG - 1) // 2) as i:
                    for g in (1, 2):
                        for c in range(2):
                            chunk(g, c, i)
                        for x in range(2):
                            lo_after(pool, down_unit(L, g - 1, x), i)
                s2 = 2 if L == 0 else 4
                for m in range(KD):
                    add_square(s2, m)
                    if m % 4 == 3:
                        lo_after(pool, down_unit(L, NG - 1, m // 4))

            ffn(0)
            with pool.Fori(0, NPAIR) as p:
                for x in range(3):
                    split_lo(pool, U_QKV + 3 + x, p, 3)
            for m in range(KD):
                lo_after(pool, U_WO + m)
                add_square(3, m)
            ffn(1)

        @block.vector
        def _(dve):
            chain = Chain(dve, v_chain)

            def opened(r, i=None, step=24):
                dve.wait_ge(full, at(r + 1, i, step))
                if i is not None or r >= 1:
                    dve.wait_ge(free, at(r, i, step))

            def emptied(r, i=None, step=24):
                dve.wait_ge(free, at(r + 1, i, step))

            def factor(r, dst, n, late=False):
                opened(r)
                if late:
                    dve.wait_ge(full, r + 2)
                dve.wait_ge(std_ok, n)
                nc.vector.reciprocal(dst, dst).then_inc(free, 1)
                emptied(r)

            def gain_lo(s, e, m):
                k = e * KD + m
                dve.wait_ge(x_hi, k + 1)
                nc.vector.scalar_tensor_tensor(out=xs[:, 1, m, :], in0=h[:, m, :], scalar=pc("g", s * KD + m),
                                               in1=xs[:, 0, m, :].bitcast(F32), op0=ALU.mult,
                                               op1=ALU.subtract).then_inc(x_lo, 1)

            def rest_lo(e, n, m, src):
                dve.wait_ge(x_hi, e * KD + n + 1)
                nc.vector.tensor_tensor(xs[:, 1, m, :], src, xs[:, 0, m, :].bitcast(F32), ALU.subtract).then_inc(x_lo, 1)

            def add_to_h(r, m, i=None):
                opened(r, i)
                nc.vector.tensor_tensor(tok(h[:, m, :]), region(r), tok(h[:, m, :]), ALU.add).then_inc(free, 1)

            for b in (g0, g1, g2, g3, sil):
                chain(nc.vector.memset(b[:, 0:PAD], 0.0))
            chain(nc.vector.memset(eps[:, 0:1], RMS_EPS))
            nc.vector.memset(eps[:, 1:2], LN_EPS).then_inc(pads_ok, 1)
            dve.wait_ge(pads_ok, 1)
            dve.wait_ge(par_in, 48)
            for m in range(KD):
                gain_lo(0, 0, m)

            def conv_tap(c, k):
                w = pc("wa", c * KA + k)
                new = AS[:, c, :, k:k + NQ]
                y = Y[c]
                ys = y[:, NP_:].rearrange("p (b q) -> p b q", b=NB)
                if k == 0:
                    nc.vector.tensor_scalar(y[:, 0:NP_], G[c][:, 0:NP_], w, pc("ba", c), ALU.mult, ALU.add).then_inc(v_chain, 1)
                    chain.n += 1
                    chain(nc.vector.tensor_scalar(ys, new, w, pc("ba", c), ALU.mult, ALU.add))
                else:
                    nc.vector.scalar_tensor_tensor(out=y[:, 0:NP_], in0=G[c][:, k:k + NP_], scalar=w, in1=y[:, 0:NP_],
                                                   op0=ALU.mult, op1=ALU.add).then_inc(v_chain, 1)
                    chain.n += 1
                    chain(nc.vector.scalar_tensor_tensor(out=ys, in0=new, scalar=w, in1=ys, op0=ALU.mult, op1=ALU.add))

            def mixer_step(kind, c, r):
                opened(r)
                if kind == "s":
                    if c > 0:
                        dve.wait_ge(sig_ok, c)
                    nc.vector.tensor_tensor(tok(tmp[:, :]), region(r), tok(rst[:, :]), ALU.mult).then_inc(free, 1)
                elif kind == "a":
                    g = G[c][:, PAD:]
                    nc.vector.tensor_tensor(tok(g), region(r), tok(rst[:, :]), ALU.mult).then_inc(free, 1)
                    emptied(r)
                    dve.wait_ge(sig_ok, c + 1)
                    chain(nc.vector.tensor_tensor(g, g, sil[:, PAD:], ALU.mult))
                    dve.wait_ge(st_in, 16 * 2 * CA)
                    chain(nc.vector.tensor_copy(AS[:, c, :, PAD:], g[:, NP_:].rearrange("p (b q) -> p b q", b=NB)))
                    nc.vector.tensor_copy(pa_st[:, c, :], G[c][:, NP_:NP_ + PAD]).then_inc(glu_ok, 1)
                    dve.wait_ge(glu_ok, c + 1)
                elif kind == "C":
                    nc.vector.tensor_tensor(tok(tmp[:, :]), region(r), tok(rst[:, :]), ALU.mult).then_inc(free, 1)
                elif kind == "X":
                    b = sil[:, PAD:]
                    nc.vector.tensor_tensor(tok(b), region(r), tok(tmp[:, :]), ALU.mult).then_inc(free, 1)
                    emptied(r)
                    chain(nc.vector.tensor_tensor(b, b, rst[:, :], ALU.mult))
                    chain(nc.vector.tensor_copy(BS[:, c, :, KB - 1:], b[:, NP_:].rearrange("p (b q) -> p b q", b=NB)))
                    chain(nc.vector.tensor_copy(pb_st[:, c, :], b[:, NP_ - KB + 1:NP_]))
                    for k in range(KB):
                        w = pc("wb", c * KB + k)
                        src = sil[:, PAD - KB + 1 + k:PAD - KB + 1 + k + NP_]
                        new = BS[:, c, :, k:k + NQ]
                        y, ys = cb[:, c, 0:NP_], cb[:, c, NP_:].rearrange("p (b q) -> p b q", b=NB)
                        if k == 0:
                            chain(nc.vector.tensor_scalar(y, src, w, None, ALU.mult))
                            chain(nc.vector.tensor_scalar(ys, new, w, None, ALU.mult))
                        else:
                            chain(nc.vector.scalar_tensor_tensor(out=y, in0=src, scalar=w, in1=y, op0=ALU.mult, op1=ALU.add))
                            chain(nc.vector.scalar_tensor_tensor(out=ys, in0=new, scalar=w, in1=ys, op0=ALU.mult, op1=ALU.add))
                    chain(nc.vector.tensor_tensor(cb[:, c, :], cb[:, c, :], rst[:, :], ALU.mult))
                else:
                    nc.vector.tensor_tensor(tok(cb[:, c, :]), region(r), tok(cb[:, c, :]), ALU.mult).then_inc(free, 1)
                    emptied(r)

            factor(NAMED["stats0"], rst[:, :], 1, late=True)
            taps = [(c, k) for c in range(CA) for k in range(KA)]
            PER = 7
            for u, (kind, c) in enumerate(MIX_ORDER):
                mixer_step(kind, c, FIRST[u])
                if u >= 1:
                    for tc, tk in taps[PER * (u - 1):PER * u]:
                        conv_tap(tc, tk)
            for tc, tk in taps[PER * 19:]:
                conv_tap(tc, tk)


            chain(nc.vector.tensor_tensor(acc[:, :], Y[0], Y[1], ALU.add))
            chain(nc.vector.tensor_tensor(acc[:, :], acc[:, :], Y[2], ALU.add))
            nc.vector.tensor_tensor(acc[:, :], acc[:, :], Y[3], ALU.add).then_inc(ysum_ok, 1)
            r = NAMED["ln_mean"]
            opened(r)
            for c in range(CA):
                if c == CA - 1:
                    dve.wait_ge(ycen_ok, c)
                ins = nc.vector.scalar_tensor_tensor(out=tok(Y[c]), in0=region(r), scalar=-2.0, in1=tok(Y[c]),
                                                     op0=ALU.mult, op1=ALU.add)
                ins.then_inc(ycen_ok if c < CA - 1 else free, 1)
            factor(NAMED["ln_var"], tmp[:, :], 2)
            for c in range(CA):
                nc.vector.tensor_tensor(Y[c], Y[c], tmp[:, :], ALU.mult).then_inc(yn_ok, 1)
            for c in range(CA):
                rest_lo(1, c, CA + c, cb[:, c, :])
            for c in range(CA):
                rest_lo(1, CA + c, c, Y[c])
            for m in range(KD):
                add_to_h(FIRST[U_OUT + m], m)

            def ffn(L):
                s, e = (1, 2) if L == 0 else (3, 5)
                for m in range(KD):
                    gain_lo(s, e, m)
                factor(NAMED[f"stats{s}"], rst[:, :], (3, 5)[L], late=True)

                def hidden_lo(g, c, i):
                    A = At(i)
                    dve.wait_ge(hid_hi, A.chunk(NJ * L + 2 * g + c + 1))
                    nc.vector.tensor_tensor(hid[:, g % 2, c, 1, :], tmp[:, :], hid[:, g % 2, c, 0, :].bitcast(F32),
                                            ALU.subtract).then_inc(hid_lo, 1)

                def chunk(g, c, i):
                    A = At(i)
                    jj = 2 * g + c
                    j = NJ * L + jj
                    rg, ru = FIRST[in_unit(L, g, 2 * c)], FIRST[in_unit(L, g, 2 * c + 1)]
                    opened(rg, i)
                    if j > 0:
                        dve.wait_ge(hist_ok, at(2 * j, i, 8))
                    nc.vector.tensor_tensor(tok(gbuf[:, PAD:]), region(rg), tok(rst[:, :]), ALU.mult).then_inc(free, 1)
                    if c == 1:
                        hidden_lo(g, 0, i)
                    emptied(rg, i)
                    if j > 0:
                        dve.wait_ge(silu_ok, A.chunk(j))
                    dj = jj if i is None else i * 4 + jj
                    for k in (KF - 1, 1, 0):
                        w = pc_dyn("wf", dj * KF + (L * NJ * KF + k))
                        src, y = gbuf[:, PAD - KF + 1 + k:PAD - KF + 1 + k + NP_], acc[:, 0:NP_]
                        if k == KF - 1:
                            chain(nc.vector.tensor_scalar(y, src, w, None, ALU.mult))
                        else:
                            chain(nc.vector.scalar_tensor_tensor(out=y, in0=src, scalar=w, in1=y, op0=ALU.mult, op1=ALU.add))
                    dve.wait_ge(hist_ok, at(2 * j + 2, i, 8))
                    y = acc[:, NP_:].rearrange("p (b q) -> p b q", b=NB)
                    for k in (KF - 1, 1, 0):
                        w = pc_dyn("wf", dj * KF + (L * NJ * KF + k))
                        if i is None:
                            src = sx[:, jj, :, k:k + NQ]
                        else:
                            src = sx[:, ds(i * 4 + jj, 1), :, k:k + NQ].rearrange("p a b q -> p (a b) q")
                        if k == KF - 1:
                            chain(nc.vector.tensor_scalar(y, src, w, None, ALU.mult))
                        else:
                            ins = nc.vector.scalar_tensor_tensor(out=y, in0=src, scalar=w, in1=y, op0=ALU.mult, op1=ALU.add)
                            if k:
                                chain(ins)
                            else:
                                ins.then_inc(conv_ok, 1)
                    opened(ru, i)
                    dve.wait_ge(silr_ok, A.chunk(j + 1))
                    if j > 0:
                        dve.wait_ge(hid_lo, A.chunk(j))
                    nc.vector.tensor_tensor(tok(tmp[:, :]), region(ru), tok(sil[:, PAD:]), ALU.mult).then_inc(free, 1)

                def group(g, i):
                    for c in range(2):
                        chunk(g, c, i)
                    if g == 0:
                        hidden_lo(0, 1, i)
                        return
                    for x in range(2):
                        u = down_unit(L, g - 1, x)
                        for m in range(4):
                            add_to_h(FIRST[u] + m, 4 * x + m, i)
                            if x == 0 and m == 0:
                                hidden_lo(g, 1, i)

                group(0, None)
                with dve.Fori(0, (NG - 1) // 2) as i:
                    chain.restart()
                    for g in (1, 2):
                        group(g, i)
                for x in range(2):
                    for m in range(4):
                        add_to_h(FIRST[down_unit(L, NG - 1, x)] + m, 4 * x + m)

            ffn(0)
            for m in range(KD):
                gain_lo(2, 3, m)
            factor(NAMED["stats2"], rst[:, :], 4)
            dve.wait_ge(st_out, 16 * (2 + 2 * CA))
            dve.wait_ge(ff_out, 16 * (1 + NB))
            chain(nc.vector.memset(qb[:, :], 0.0))
            nc.vector.memset(qa[:, :], 0.0).then_inc(so_free, 1)
            dve.wait_ge(so_free, 1)
            nc.vector.memset(spT[:, :, :], 0.0).then_inc(o_free, 1)
            dve.wait_ge(o_free, 1)
            dve.wait_ge(kv_out, 16)
            dve.wait_ge(x_lo, 4 * KD)
            dve.wait_ge(x_hi, 4 * KD)
            r0 = FIRST[U_QKV]
            with dve.Fori(0, NPAIR) as p:
                chain.restart()

                def wait(s, step, base):
                    dve.wait_ge(s, (p if step == 1 else p * step) + base)

                def settle():
                    chain(nc.vector.tensor_copy(eps[0:1, 2:3], eps[0:1, 0:1]))

                opened(r0, p, 20)
                nc.vector.scalar_tensor_tensor(out=tok(QT[:, :]), in0=region(r0), scalar=HD ** -0.5, in1=tok(rst[:, :]),
                                               op0=ALU.mult, op1=ALU.mult).then_inc(free, 1)
                emptied(r0, p, 20)
                for hh in range(2):
                    rows = slice(HD * hh, HD * hh + HD)
                    src = QT[rows, NP_:].rearrange("p (b q) -> p b q", b=NB)
                    qb_v = qb[rows, :].rearrange("p (b s) -> p b s", s=72)[:, :, NQ * hh:NQ * hh + NQ]
                    qa_v = qa[rows, :].rearrange("p (b s) -> p b s", s=8)[:, :, NQ * hh:NQ * hh + NQ]
                    chain(nc.vector.tensor_copy(qb_v, src))
                    ins = nc.vector.tensor_copy(qa_v, src)
                    if hh == 0:
                        chain(ins)
                    else:
                        ins.then_inc(q_ok, 1)
                opened(r0 + 1, p, 20)
                wait(kv_out, 32, 16)
                nc.vector.tensor_tensor(tok(KT[:, :]), region(r0 + 1), tok(rst[:, :]), ALU.mult).then_inc(free, 1)
                opened(r0 + 2, p, 20)
                nc.vector.tensor_tensor(tok(VT[:, :]), region(r0 + 2), tok(rst[:, :]), ALU.mult).then_inc(free, 1)

                wait(ss_full, 1, 1)
                wait(sb_in, 16, 16)
                settle()
                nc.vector.tensor_tensor_reduce(out=sps[:, :], in0=ob[0:64, :, :].rearrange("p a c -> p (a c)")[:, 0:NKEYS],
                                               in1=sps[:, :], scale=-1.0, scalar=3.0e38, op0=ALU.add, op1=ALU.min,
                                               accum_out=snm[:, 0:1]).then_inc(ss_free, 1)
                opened(r0 + 3, p, 20)
                vr = reg[(r0 + 3) % 2]
                chain(nc.vector.tensor_copy(vrow[:, :, :], vr[:, 0:2, :].rearrange("p a (t c) -> p (a t) c", c=P)))
                nc.vector.tensor_copy(vnew[:, :], vr[0:NS, 2, 0:P]).then_inc(free, 1)

                def neg_scores(n):
                    hh, b = n // 8, n % 8
                    r = r0 + 4 + n
                    opened(r, p, 20)
                    if b == 0:
                        wait(wt_in[hh], 16, 16)
                    w = P * (b + 1)
                    settle()
                    nc.vector.tensor_tensor_reduce(out=neg_s[:, n % 2, 0:w],
                                                   in0=reg[r % 2][:, 0:2, :].rearrange("p a c -> p (a c)")[:, 0:w],
                                                   in1=wt[:, hh, 1024 - w:1024], scale=-1.0, scalar=3.0e38,
                                                   op0=ALU.add, op1=ALU.min, accum_out=nmx[:, n:n + 1]).then_inc(free, 1)

                def norm(n):
                    w = P * (n % 8 + 1)
                    wait(exp_ok, 16, n + 1)
                    chain(nc.vector.reciprocal(lsum[:, 1, n:n + 1], lsum[:, 0, n:n + 1]))
                    nc.vector.tensor_scalar(neg_s[:, n % 2, 0:w], neg_s[:, n % 2, 0:w], lsum[:, 1, n:n + 1], None,
                                            ALU.mult).then_inc(p_ok, 1)

                neg_scores(0)
                wait(sp_exp, 1, 1)
                chain(nc.vector.reciprocal(snm[:, 2:3], snm[:, 1:2]))
                nc.vector.tensor_scalar(sps[:, :], sps[:, :], snm[:, 2:3], None, ALU.mult).then_inc(sp_ok, 1)
                neg_scores(1)
                norm(0)
                for n in range(16):
                    b = n % 8
                    if n + 1 < 16:
                        norm(n + 1)
                    wait(pt_full, 16, n + 1)
                    k = min(b + 1, 4)
                    nc.vector.tensor_copy(pT[:, 0:k, :], reg[0][:, 2, 0:P * k].rearrange("p (k q) -> p k q", q=P)).then_inc(pt_a, 1)
                    if n + 2 < 16:
                        neg_scores(n + 2)
                    if n == 11:
                        wait(so_full, 1, 1)
                        for hh in range(2):
                            rows = slice(HD * hh, HD * hh + HD)
                            dst = att[rows, ds(p, 1), NP_:].rearrange("p a (b q) -> p (a b) q", b=NB)
                            src = reg[1][rows, 2, 256:512].rearrange("p (b r) -> p b r", b=NB)[:, :, NQ * hh:NQ * hh + NQ]
                            ins = nc.vector.tensor_copy(dst, src)
                            if hh == 0:
                                chain(ins)
                            else:
                                ins.then_inc(so_free, 1)
            dve.wait_ge(o_free, 1 + 4 * NPAIR)
            dve.wait_ge(so_free, NPAIR + 1)
            for m in range(KD):
                rest_lo(4, m, m, att[:, m, :])
            dve.wait_ge(kv_out, 16 + 32 * NPAIR)
            chain(nc.vector.memset(g3[:, 0:PAD], 0.0))
            dve.wait_ge(h_back, 16)
            for m in range(KD):
                add_to_h(FIRST[U_WO + m], m)
            ffn(1)
            factor(NAMED["stats4"], rst[:, :], 6)
            for m in range(KD):
                nc.vector.scalar_tensor_tensor(out=h[:, m, :], in0=h[:, m, :], scalar=pc("g", 4 * KD + m), in1=rst[:, :],
                                               op0=ALU.mult, op1=ALU.mult).then_inc(y_ok, 1)
    return nc


def branch_bias(dist, slope):
    count = sum((((dist >= 0) & (dist <= w) & (dist % d == 0)).astype(np.float32) for w, d in BRANCHES))
    return np.where(count > 0, -slope * dist.astype(np.float32) + np.log(np.maximum(count, 1)), MASKED).astype(np.float32)


def bias_tables():
    slopes = (2.0 ** (-8.0 * np.arange(1, NH + 1) / NH)).astype(np.float32)
    dist = np.arange(P)[:, None] + (NP_ - P) - np.arange(NP_)[None, :]
    prompt = np.zeros((NH + 2, P, NP_), np.float32)
    for hd in range(NH):
        prompt[hd] = branch_bias(dist, slopes[hd])
    pos = key_positions()
    sample = np.zeros((NPAIR + 1, NB, 2, NQ, NKEYS), np.float32)
    for hd in range(NH):
        for j in range(NQ):
            s = sample[hd // 2, :, hd % 2, j]
            s[:, :NKEY] = branch_bias(PAST + j - pos, slopes[hd])
            s[:, NKEY:] = MASKED
            for b in range(NB):
                s[b, NKEY + NQ * b:NKEY + NQ * (b + 1)] = branch_bias(j - np.arange(NQ), slopes[hd])
    return prompt, sample.reshape(NPAIR + 1, 2 * NS, NKEYS)


def key_positions():
    far = (16 * np.arange((PAST - 512) // 16)[:, None] + np.arange(NQ)[None, :]).ravel()
    return np.concatenate([far, np.arange(PAST - 512, PAST)])


def kernel(**inputs):
    import concourse.bacc as bacc
    from concourse.bass_utils import run_bass_kernel_spmd

    a = {k: np.asarray(v) for k, v in inputs.items()}

    def chunks(x):
        n = x.shape[-1] // P
        y = x.reshape(x.shape[:-1] + (n, P))
        return np.ascontiguousarray(np.moveaxis(np.moveaxis(y, -1, 0), -1, 1))

    xT = np.concatenate([chunks(a["x_prompt"][0]), chunks(a["x_sample"].reshape(NS, D))], axis=2)

    def col_unit(w, col):
        return w[:, col:col + P].reshape(KD, P, P).transpose(1, 0, 2).reshape(P, 1024)

    def row_unit(w, g, half):
        return w[2 * P * g:2 * P * (g + 1), 512 * half:512 * half + 512].reshape(2, P, 512).transpose(1, 0, 2).reshape(P, 1024)

    units = []
    starts = {"a": 0, "s": 512, "G": 1024, "C": 1536, "X": 2048}
    for kind, c in MIX_ORDER:
        units.append(col_unit(a["w_in_ab"][0], starts[kind] + P * c))
    for m in range(KD):
        units.append(col_unit(a["w_out_ab"][0], P * m))

    def ffn_units(L):
        w_in, w_dn, out = a["w_ffn_in"][L], a["w_down"][L], []
        for g in range(NG):
            for c in range(2):
                out += [col_unit(w_in, P * (2 * g + c)), col_unit(w_in, DFF + P * (2 * g + c))]
            if g > 0:
                out += [row_unit(w_dn, g - 1, x) for x in range(2)]
        return out + [row_unit(w_dn, NG - 1, x) for x in range(2)]

    units += ffn_units(0)
    for p in range(NPAIR):
        units += [col_unit(a["w_qkv"][0], x * D + P * p) for x in range(3)]
    for m in range(KD):
        units.append(col_unit(a["w_o"][0], P * m))
    units += ffn_units(1)
    wstream = np.stack(units + [np.zeros_like(units[0])])

    def flat(x):
        return x.reshape(P, -1)

    par = np.concatenate([
        flat(np.moveaxis(chunks(np.stack([a["g_mix"][0], a["g_ffn"][0], a["g_mix"][1], a["g_ffn"][1], a["g_final"]])), 2, 1)),
        flat(chunks(a["conv_a_w"][0])), flat(chunks(a["conv_a_b"][0])), flat(chunks(a["ln_a_g"][0])),
        flat(chunks(a["ln_a_b"][0])), flat(chunks(a["conv_b_w"][0])),
        flat(np.moveaxis(chunks(a["conv_f_w"]), 2, 1)),
    ], axis=1)

    pos = key_positions()
    kg = a["cache_k"][0][:, pos].reshape(NB, NKEY, NPAIR, P)
    vg = a["cache_v"][0][:, pos].reshape(NB, KT_TILES, P, NPAIR, P)
    kv = np.concatenate([kg.transpose(2, 0, 3, 1), vg.transpose(3, 0, 2, 1, 4).reshape(NPAIR, NB, P, NKEY)], axis=1)
    wtab, sbias = bias_tables()
    arrays = {
        "xT": xT, "wstream": wstream, "par": par, "ident": np.eye(P, dtype=np.float32),
        "ones": np.full((P, P), 1.0 / D, np.float32),
        "stA": chunks(a["state_conv_a"][0]), "stB": chunks(a["state_conv_b"][0]),
        "stF": np.ascontiguousarray(np.moveaxis(chunks(a["state_ffn"]), 2, 0)),
        "kv": kv, "wtab": wtab, "sbias": sbias,
        "cache_k": a["cache_k"][0].reshape(NB, PAST * D), "cache_v": a["cache_v"][0].reshape(NB, PAST * D),
    }
    outs = {
        "y": (P, KD, T), "pA": (P, CA, PAD), "sA": (P, CA, NB, PAD), "pB": (P, CA, KB - 1), "sB": (P, CA, NB, KB - 1),
        "kT": (NPAIR, P, T), "vT": (NPAIR, P, T), "sk": (NB, KEPT * D), "sv": (NB, KEPT * D),
        "pF": (2, P, NJ, KF - 1), "sF": (2, P, NJ, NB, KF - 1),
    }
    nc = bacc.Bacc("TRN2", target_bir_lowering=False, num_devices=1)
    arrays = {f"in_{k}": np.ascontiguousarray(v) for k, v in arrays.items()}
    ins = [nc.dram_tensor(k, v.shape, F32, kind="ExternalInput").ap() for k, v in arrays.items()]
    spill = nc.dram_tensor("h_spill", (P, KD, T), F32, kind="Internal").ap()
    res = [nc.dram_tensor(f"out_{k}", s, F32, kind="ExternalOutput").ap() for k, s in outs.items()]
    build(nc, *ins, spill, *res)
    r = run_bass_kernel_spmd(nc, [arrays], core_ids=[0]).results[0]
    o = {k: np.asarray(r[f"out_{k}"]) for k in outs}

    def rows(x):
        y = np.moveaxis(np.moveaxis(x, 1, -1), 0, -1)
        return y.reshape(y.shape[:-2] + (-1,))

    y = rows(o["y"])
    kT, vT = (o[k].transpose(2, 0, 1).reshape(T, D) for k in ("kT", "vT"))

    def cache(kept, new):
        return np.concatenate([kept.reshape(NB, KEPT, NH, HD), new.reshape(NB, NQ, NH, HD)], axis=1)[None]

    return (y[:NP_][None], y[NP_:].reshape(NB, NQ, D),
            rows(o["pA"])[None, None], rows(o["sA"])[None],
            rows(o["pB"])[None, None], rows(o["sB"])[None],
            kT[:NP_].reshape(1, 1, NP_, NH, HD), cache(o["sk"], kT[NP_:]),
            vT[:NP_].reshape(1, 1, NP_, NH, HD), cache(o["sv"], vT[NP_:]),
            np.stack([rows(x)[None] for x in o["pF"]]), np.stack([rows(x) for x in o["sF"]]))
```

```python
from contextlib import ExitStack

import numpy as np
import concourse.bass as bass
from concourse import mybir

F32 = mybir.dt.float32
F32R = mybir.dt.float32r
ALU = mybir.AluOpType
ACT = mybir.ActivationFunctionType
ds = bass.ds

P = 128
D = 1024
KD = D // P
NP_, NB, NQ = 1024, 8, 4
NS = NB * NQ
T = NP_ + NS
NT, TS = 3, T // 3
CA = 4
KA, KB, KF = 31, 3, 3
PAD = KA - 1
DFF = 2816
NJ = DFF // P
NG = NJ // 2
NH, HD = 16, 64
NPAIR = NH // 2
PAST = 2048
NKEY = 896
KT_TILES = NKEY // P
NKEYS = NKEY + NS
MASKED = -1.0e30
BRANCHES = ((128, 1), (512, 4), (2048, 16))
LN_EPS, RMS_EPS = 1e-5, 1e-6
KEPT = PAST - NQ

U_IN, U_OUT, U_FFN, U_QKV, U_WO = 0, 20, (28, 126), 94, 118
NUNITS = 192
MIX_ORDER = []
for _c in range(CA):
    MIX_ORDER += [("s", _c), ("a", _c)]
for _c in range(CA):
    MIX_ORDER += [("C", _c), ("X", _c), ("G", _c)]


def plan_uses():
    first, last, named, n = {}, {}, {}, 0

    def unit(u, k=1):
        nonlocal n
        first[u], last[u] = n, n + k - 1
        n += k

    def name(key, k=1):
        nonlocal n
        named[key] = n
        n += k

    unit(0)
    for u in range(1, 20):
        unit(u)
    name("ln_mean")
    name("ln_var")
    for u in range(20, 28):
        unit(u)
    for layer in range(2):
        if layer == 1:
            name("stats2")
            for p in range(NPAIR):
                for x in range(3):
                    unit(U_QKV + 3 * p + x)
                name(("vrows", p))
                name(("scores", p), 16)
            for m in range(KD):
                unit(U_WO + m)
        u = U_FFN[layer]
        unit(u)
        for x in range(1, 4):
            unit(u + x)
        u += 4
        for _g in range(1, NG):
            for x in range(4):
                unit(u + x)
            for x in range(2):
                unit(u + 4 + x, 4)
            u += 6
        for x in range(2):
            unit(u + x, 4)
    name("stats4")
    return first, last, named


FIRST, LAST, NAMED = plan_uses()
BLOCKS = ((0, 7), (0, 0), (1, 7), (1, 0), (0, 6), (0, 1), (1, 6), (1, 1),
          (0, 5), (0, 2), (1, 5), (1, 2), (0, 4), (1, 4), (0, 3), (1, 3))
SAMPLE_STEPS = {9: (0, 1, 2), 11: (3, 4, 5), 14: (6, 7)}
SQ0 = {0: 0, "ln": 8, 1: 12, 2: 20, 3: 28, 4: 36}


def at(base, i, step):
    return base if i is None else i * step + base


def build(nc, xT, wstream, par, ident_d, ones_d, stA, stB, stF, kv, wtab, sbias, cache_k, cache_v,
          h_spill, o_y, o_pA, o_sA, o_pB, o_sB, o_kT, o_vT, o_sk, o_sv, o_pF, o_sF):
    base0 = (nc.sbuf_base + 31) // 32 * 32

    with ExitStack() as ctx:
        def place(name, shape, dt, off):
            size = int(np.prod(shape[1:])) * 4
            return nc.alloc_sbuf_tensor_at(name, shape, dt, offset=off), off + (size + 31) // 32 * 32

        def sem(name):
            return ctx.enter_context(nc.semaphore(name))

        off = base0
        H0 = off
        h, off = place("h", [P, KD, T], F32, off)
        X0 = off
        xs, off = place("xs", [P, 2, KD, T], F32R, off)
        M0 = off
        hid, off = place("hid", [P, 2, 2, 2, T], F32R, off)
        w_raw, off = place("w_raw", [P, 3, 1024], F32, off)
        w_sp, off = place("w_sp", [P, 3, 2, 1024], F32R, off)
        T0 = off
        rst, off = place("rst", [P, T], F32, off)
        ident, off = place("ident", [P, P], F32, off)
        ones, off = place("ones", [P, P], F32, off)
        NPAR = par.shape[1]
        pt, off = place("pt", [P, NPAR], F32, off)
        eps, off = place("eps", [P, 4], F32, off)
        T1 = off
        BS, off = place("BS", [P, CA, NB, KB - 1 + NQ], F32, off)
        pa_st, off = place("pa_st", [P, CA, PAD], F32, off)
        pb_st, off = place("pb_st", [P, CA, KB - 1], F32, off)
        sx, off = place("sx", [P, NJ, NB, KF - 1 + NQ], F32, off)
        pf_st, off = place("pf_st", [P, NJ, KF - 1], F32, off)
        g3, off = place("g3", [P, PAD + T], F32, off)
        spare, off = place("spare", [P, T], F32, off)
        AS, off = place("AS", [P, CA, NB, PAD + NQ], F32, off)
        tmp, off = place("tmp", [P, T], F32, off)
        sil, off = place("sil", [P, PAD + T], F32, off)
        acc, off = place("acc", [P, T], F32, off)
        prod, off = place("prod", [P, 2, NB, KA], F32, off)
        assert off <= nc.sbuf_usable_end
        gbuf = g3
        g0, o2 = place("g0", [P, PAD + T], F32, M0)
        g1, o2 = place("g1", [P, PAD + T], F32, o2)
        g2, o2 = place("g2", [P, PAD + T], F32, o2)
        cb, o2 = place("cb", [P, CA, T], F32, o2)
        assert o2 <= M0 + 2 * 2 * 2 * T * 4
        G = [g0, g1, g2, g3]
        Y = [spare[:, :], g0[:, PAD:], g1[:, PAD:], g2[:, PAD:]]
        att, _ = place("att", [P, KD, T], F32, M0)
        neg_s, o2 = place("neg_s", [P, 3, 1024], F32, H0)
        kvr, o2 = place("kvr", [P, 4, NKEY], F32, o2)
        vrow, o2 = place("vrow", [P, 8, P], F32, o2)
        so, o2 = place("so", [P, 2, P], F32, o2)
        vnew, o2 = place("vnew", [NS, P], F32, o2)
        nmx, o2 = place("nmx", [P, 16], F32, o2)
        lsum, o2 = place("lsum", [P, 2, 16], F32, o2)
        snm, o2 = place("snm", [64, 8], F32, o2)
        assert o2 <= X0
        wt, o2 = place("wt", [P, 2, 1024], F32, T1)
        QT, o2 = place("QT", [P, T], F32, o2)
        KT, o2 = place("KT", [P, T], F32, o2)
        VT, o2 = place("VT", [P, T], F32, o2)
        pT, o2 = place("pT", [P, 8, P], F32, o2)
        spT, o2 = place("spT", [P, 8, 88], F32, o2)
        qb, o2 = place("qb", [P, 8 * 72], F32, o2)
        qa, o2 = place("qa", [P, 64], F32, o2)
        sps, o2 = place("sps", [64, NKEYS], F32, o2)
        assert o2 <= nc.sbuf_usable_end

        reg = [ctx.enter_context(nc.psum_tensor(f"reg{i}", [P, 3, 512], F32)) for i in range(2)]
        ob = ctx.enter_context(nc.psum_tensor("ob", [P, 2, 512], F32))

        def region(use):
            return reg[use % 2][:, :, 0:TS]

        def tok(ap):
            return ap.rearrange("p (s t) -> p s t", s=NT)

        cols, c0 = {}, 0
        for key, n in (("g", 5 * KD), ("wa", CA * KA), ("ba", CA), ("lg", CA), ("lb", CA), ("wb", CA * KB),
                       ("wf", 2 * NJ * KF)):
            cols[key] = c0
            c0 += n

        def pc(key, idx):
            return pt[:, cols[key] + idx:cols[key] + idx + 1]

        def pc_dyn(key, idx):
            return pt[:, ds(idx + cols[key], 1)] if not isinstance(idx, int) else pc(key, idx)

        par_in, ident_in, st_in, sx_in = (sem(s) for s in ("par_in", "ident_in", "st_in", "sx_in"))
        h_in = [sem(f"h_in{i}") for i in range(4)]
        w_in = [sem(f"w_in{i}") for i in range(3)]
        kv_in = [sem(f"kv_in{i}") for i in range(4)]
        wt_in = [sem(f"wt_in{i}") for i in range(2)]
        sb_in, h_back, kv_out = sem("sb_in"), sem("h_back"), sem("kv_out")
        copied, st_out, ff_out, y_out = sem("copied"), sem("st_out"), sem("ff_out"), sem("y_out")
        w_hi, w_lo = sem("w_hi"), sem("w_lo")
        full, free = sem("region_full"), sem("region_free")
        x_hi, x_lo = sem("x_hi"), sem("x_lo")
        sq_ok, sum_ok, st_full, std_ok = (sem(s) for s in ("sq_ok", "sum_ok", "st_full", "std_ok"))
        sig_ok, glu_ok, ysum_ok, ycen_ok, yn_ok = (sem(s) for s in ("sig_ok", "glu_ok", "ysum_ok", "ycen_ok", "yn_ok"))
        pads_ok = sem("pads_ok")
        sigr_ok, cr_ok, cb_ok, cbr_ok = (sem(s) for s in ("sigr_ok", "cr_ok", "cb_ok", "cbr_ok"))
        conv_ok, silu_ok, silr_ok, hist_ok = (sem(s) for s in ("conv_ok", "silu_ok", "silr_ok", "hist_ok"))
        hid_hi, hid_lo = sem("hid_hi"), sem("hid_lo")
        y_ok = sem("y_ok")
        q_ok, ss_full, ss_free = sem("q_ok"), sem("ss_full"), sem("ss_free")
        kv_used, exp_ok, p_ok, pt_full, pt_a, pt_b, pv_ok, o_free = (
            sem(s) for s in ("kv_used", "exp_ok", "p_ok", "pt_full", "pt_a", "pt_b", "pv_ok", "o_free"))
        sp_exp, sp_ok, spt_full, spt_ok = (sem(s) for s in ("sp_exp", "sp_ok", "spt_full", "spt_ok"))
        so_ok, so_full, so_free = (sem(s) for s in ("so_ok", "so_full", "so_free"))
        v_chain, a_chain, g_chain = sem("v_chain"), sem("a_chain"), sem("g_chain")

        class Chain:

            def __init__(self, eng, s):
                self.eng, self.s, self.n = eng, s, 0

            def __call__(self, ins):
                ins.then_inc(self.s, 1)
                self.n += 1
                self.eng.wait_ge(self.s, self.n)

            def restart(self):
                self.eng.sem_clear(self.s)
                self.n = 0

        def in_unit(L, g, x):
            return U_FFN[L] + (x if g == 0 else 6 * g - 2 + x)

        def down_unit(L, g, x):
            return U_FFN[L] + (6 * (g + 1) + 2 + x if g < NG - 1 else 64 + x)

        class At:

            def __init__(self, i):
                self.i = i

            def unit(self, u):
                return at(u, self.i, 12)

            def use(self, r):
                return at(r, self.i, 24)

            def chunk(self, j):
                return at(j, self.i, 4)

        def load_unit(sp, u, slot, i=None, step=3):
            if i is not None or u >= 3:
                sp.wait_ge(w_lo, at(u - 2, i, step))
            src = wstream[u] if i is None else wstream[ds(i * step + u, 1), :, :].rearrange("a p c -> (a p) c")
            sp.dma_start(w_raw[:, slot, :], src).then_inc(w_in[slot], 16)

        def split_hi(act, u, i=None, step=12, used=None):
            act.wait_ge(w_in[u % 3], at(16 * (u // 3 + 1), i, 16 * step // 3))
            if used is not None:
                act.wait_ge(full, used)
            nc.scalar.activation(w_sp[:, u % 3, 0, :], w_raw[:, u % 3, :], ACT.Copy).then_inc(w_hi, 1)

        def split_lo(pool, u, i=None, step=12):
            pool.wait_ge(w_hi, at(u + 1, i, step))
            nc.gpsimd.tensor_tensor(w_sp[:, u % 3, 1, :], w_raw[:, u % 3, :], w_sp[:, u % 3, 0, :].bitcast(F32),
                                    ALU.subtract).then_inc(w_lo, 1)

        def hi_after(act, u, i=None, step=12, ustep=24):
            if u + 3 < NUNITS:
                split_hi(act, u + 3, i, step, at(LAST[u] + 1, i, ustep))

        def lo_after(pool, u, i=None, step=12):
            if u + 3 < NUNITS:
                split_lo(pool, u + 3, i, step)

        def h_ready(eng, s, m):
            if s == 0:
                eng.wait_ge(h_in[m // 2], 16)
            elif s == 1:
                eng.wait_ge(free, FIRST[U_OUT + m] + 1)
            elif s == 3:
                eng.wait_ge(free, FIRST[U_WO + m] + 1)
            else:
                L = 0 if s == 2 else 1
                eng.wait_ge(free, FIRST[down_unit(L, NG - 1, m // 4)] + m % 4 + 1)

        sqb = [sil[:, PAD:], tmp[:, :]]

        block = ctx.enter_context(nc.Block())

        @block.sync
        def _(sp):
            sp.dma_start(pt[:], par).then_inc(par_in, 16)
            load_unit(sp, 0, 0)
            for q in range(4):
                sp.dma_start(h[:, 2 * q:2 * q + 2, :], xT[:, 2 * q:2 * q + 2, :]).then_inc(h_in[q], 16)
                if q in (1, 2):
                    load_unit(sp, q, q)
                if q == 0:
                    for dst, src in ((ident, ident_d), (ones, ones_d)):
                        sp.dma_start(dst[:], src).then_inc(ident_in, 16)
            for c in range(CA):
                sp.dma_start(AS[:, c, :, 0:PAD], stA[:, c]).then_inc(st_in, 16)
                sp.dma_start(BS[:, c, :, 0:KB - 1], stB[:, c]).then_inc(st_in, 16)
            for b in range(NB):
                sp.dma_start(sx[:, :, b, 0:KF - 1], stF[0, :, :, b]).then_inc(sx_in, 16)

            def copy_piece(b, x):
                cache, out = ((cache_k, o_sk), (cache_v, o_sv))[x // 2]
                half, n = x % 2, KEPT * D // 2
                if isinstance(b, int):
                    src, dst = cache[b], out[b]
                else:
                    src = cache[ds(b, 1), :].rearrange("a n -> (a n)")
                    dst = out[ds(b, 1), :].rearrange("a n -> (a n)")
                src = src[NQ * D + half * n:NQ * D + (half + 1) * n].rearrange("(e r c) -> e r c", e=16, c=896)
                dst = dst[half * n:(half + 1) * n].rearrange("(e r c) -> e r c", e=16, c=896)
                sp.dma_start(dst, src).then_inc(copied, 16)

            with sp.Fori(0, NB - 1) as i:
                for x in range(4):
                    for s in range(3):
                        load_unit(sp, 3 + 3 * x + s, s, i, 12)
                    copy_piece(i, x)
            for x in range(4):
                for s in range(3):
                    if 87 + 3 * x + s <= 94:
                        load_unit(sp, 87 + 3 * x + s, s)
                copy_piece(NB - 1, x)
            sp.wait_ge(ysum_ok, 1)
            sp.dma_start(o_pA, pa_st[:]).then_inc(st_out, 16)
            sp.dma_start(o_pB, pb_st[:]).then_inc(st_out, 16)
            for c in range(CA):
                sp.dma_start(o_sA[:, c], AS[:, c, :, NQ:]).then_inc(st_out, 16)
                sp.dma_start(o_sB[:, c], BS[:, c, :, NQ:]).then_inc(st_out, 16)

            def store_ffn_state(L):
                sp.wait_ge(hist_ok, 2 * NJ * (L + 1))
                sp.dma_start(o_pF[L], pf_st[:]).then_inc(ff_out, 16)
                for b in range(NB):
                    sp.dma_start(o_sF[L, :, :, b], sx[:, :, b, NQ:]).then_inc(ff_out, 16)

            store_ffn_state(0)
            load_unit(sp, 95, 2)
            load_unit(sp, 96, 0)
            for m in range(KD):
                h_ready(sp, 2, m)
            sp.dma_start(h_spill, h[:]).then_inc(kv_out, 16)
            sp.wait_ge(kv_out, 16)
            sp.wait_ge(x_lo, 8 * 4)
            sp.wait_ge(x_hi, 8 * 4)
            sp.wait_ge(sum_ok, SQ0[2] + KD)
            sp.wait_ge(ff_out, 16 * (1 + NB))
            sp.wait_ge(st_out, 16 * (2 + 2 * CA))
            sp.wait_ge(free, NAMED["stats2"] + 1)
            for hh in range(2):
                sp.dma_start(wt[:, hh, :], wtab[hh]).then_inc(wt_in[hh], 16)
            sp.dma_start(sps[:], sbias[0]).then_inc(sb_in, 16)

            def kv_item(p, x):
                src = kv[ds(p, 1), x].rearrange("a p c -> (a p) c")
                sp.dma_start(kvr[:, x % 4, :], src).then_inc(kv_in[x % 4], 16)

            r0 = FIRST[U_QKV]
            with sp.Fori(0, NPAIR) as p:
                sp.wait_ge(so_free, p + 1)
                for x in range(16):
                    if x == 4:
                        for y in range(3):
                            load_unit(sp, 97 + y, (97 + y) % 3, p, 3)
                        sp.wait_ge(free, p * 20 + (r0 + 2))
                        sp.dma_start(o_kT[ds(p, 1)].rearrange("a p c -> (a p) c"), KT[:]).then_inc(kv_out, 16)
                        sp.wait_ge(free, p * 20 + (r0 + 3))
                        sp.dma_start(o_vT[ds(p, 1)].rearrange("a p c -> (a p) c"), VT[:]).then_inc(kv_out, 16)
                    if x >= 4:
                        sp.wait_ge(kv_used, p * 16 + (x - 3))
                    kv_item(p, x)
                sp.wait_ge(free, p * 20 + (r0 + 4 + 15))
                sp.dma_start(wt[:, 0, :], wtab[ds(p * 2 + 2, 1)].rearrange("a p c -> (a p) c")).then_inc(wt_in[0], 16)
                sp.wait_ge(free, p * 20 + (r0 + 4 + 16))
                sp.dma_start(wt[:, 1, :], wtab[ds(p * 2 + 3, 1)].rearrange("a p c -> (a p) c")).then_inc(wt_in[1], 16)
                sp.wait_ge(spt_full, p + 1)
                sp.dma_start(sps[:], sbias[ds(p + 1, 1)].rearrange("a p c -> (a p) c")).then_inc(sb_in, 16)
            sp.wait_ge(so_free, NPAIR + 1)
            sp.wait_ge(o_free, 1 + 2 * NPAIR)
            sp.wait_ge(free, r0 + 20 * NPAIR)
            sp.wait_ge(wt_in[0], 16 * (NPAIR + 1))
            sp.wait_ge(wt_in[1], 16 * (NPAIR + 1))
            sp.wait_ge(sb_in, 16 * (NPAIR + 1))
            sp.wait_ge(kv_out, 16 + 32 * NPAIR)
            sp.dma_start(h[:], h_spill).then_inc(h_back, 16)
            for b in range(NB):
                sp.dma_start(sx[:, :, b, 0:KF - 1], stF[1, :, :, b]).then_inc(sx_in, 16)
            n_left = NUNITS + 1 - 121
            with sp.Fori(0, n_left // 3) as i:
                for s in range(3):
                    load_unit(sp, 121 + s, (121 + s) % 3, i, 3)
            for s in range(n_left % 3):
                load_unit(sp, 121 + n_left // 3 * 3 + s, (121 + n_left // 3 * 3 + s) % 3)
            store_ffn_state(1)
            for m in range(KD):
                sp.wait_ge(y_ok, m + 1)
                sp.dma_start(o_y[:, m], h[:, m, :]).then_inc(y_out, 16)
            sp.wait_ge(copied, 16 * 4 * NB)
            sp.wait_ge(st_out, 16 * (2 + 2 * CA))
            sp.wait_ge(ff_out, 2 * 16 * (1 + NB))
            sp.wait_ge(y_out, 16 * KD)

        @block.tensor
        def _(pe):
            def open_use(r, i=None, step=24):
                if i is not None or r >= 2:
                    pe.wait_ge(free, at(r - 1, i, step))

            def in_proj(u, r, i=None, ustep=12, rstep=24, x_at=None, order=range(KD), part=range(KD), midway=None):
                pe.wait_ge(w_lo, at(u + 1, i, ustep))
                open_use(r, i, rstep)
                out = region(r)
                w = w_sp[:, u % 3]
                for n in part:
                    k = order[n]
                    if midway and n == KD // 2:
                        midway()
                    if x_at is not None:
                        pe.wait_ge(x_lo, x_at + n + 1)
                    for wh, xh in ((0, 0), (0, 1), (1, 0)):
                        for t in range(NT):
                            mm = nc.tensor.matmul(out[:, t, :], w[:, wh, k * P:(k + 1) * P],
                                                  xs[:, xh, k, t * TS:(t + 1) * TS],
                                                  start=(n == 0 and wh + xh == 0), stop=(n == KD - 1 and wh == 1))
                if KD - 1 in part:
                    mm.then_inc(full, 1)

            def down_proj(u, r, par_g, i=None):
                pe.wait_ge(w_lo, at(u + 1, i, 12))
                w = w_sp[:, u % 3]
                for m in range(4):
                    open_use(r + m, i)
                    out = region(r + m)
                    for kk in range(2):
                        for wh, xh in ((0, 0), (0, 1), (1, 0)):
                            for t in range(NT):
                                mm = nc.tensor.matmul(out[:, t, :], w[:, wh, kk * 512 + m * P:kk * 512 + (m + 1) * P],
                                                      hid[:, par_g, kk, xh, t * TS:(t + 1) * TS],
                                                      start=(kk == 0 and wh + xh == 0), stop=(kk == 1 and wh == 1))
                    mm.then_inc(full, 1)

            def column_means(r, ready, src):
                pe.wait_ge(*ready)
                open_use(r)
                for t in range(NT):
                    mm = nc.tensor.matmul(region(r)[:, t, :], ones[:, :], src[:, t * TS:(t + 1) * TS],
                                          start=True, stop=True)
                mm.then_inc(full, 1)

            def first_units(s, n, u, x_at):
                in_proj(u, FIRST[u], x_at=x_at)
                pe.wait_ge(sum_ok, SQ0[s] + KD)
                for x in range(2):
                    mm = nc.tensor.matmul(ob[:, x, :], ones[:, :], acc[:, 512 * x:512 * x + 512], start=True, stop=True)
                mm.then_inc(st_full, 1)

                def sample_tokens():
                    pe.wait_ge(std_ok, n - 1)
                    nc.tensor.matmul(ob[:, 0, 0:NS], ones[:, :], acc[:, NP_:], start=True, stop=True).then_inc(st_full, 1)

                in_proj(u + 1, FIRST[u + 1], midway=sample_tokens)

            pe.wait_ge(ident_in, 32)
            first_units(0, 2, 0, 0)
            with pe.Fori(0, 3) as i:
                for x in range(6):
                    in_proj(2 + x, FIRST[2 + x], i, 6, 6)
            mix = (4, 5, 6, 7, 0, 1, 2, 3)
            column_means(NAMED["ln_mean"], (ysum_ok, 1), acc)
            in_proj(U_OUT, FIRST[U_OUT], x_at=KD, order=mix, part=range(4))
            column_means(NAMED["ln_var"], (sum_ok, SQ0["ln"] + CA), acc)
            in_proj(U_OUT + 1, FIRST[U_OUT + 1], order=mix, part=range(4))
            in_proj(U_OUT, FIRST[U_OUT], x_at=KD, order=mix, part=range(4, 8))
            in_proj(U_OUT + 1, FIRST[U_OUT + 1], order=mix, part=range(4, 8))
            for m in range(2, KD):
                in_proj(U_OUT + m, FIRST[U_OUT + m], order=mix)

            def ffn(L):
                s, e = (1, 2) if L == 0 else (3, 5)
                first_units(s, (5, 8)[L], in_unit(L, 0, 0), e * KD)
                for x in range(2, 4):
                    in_proj(in_unit(L, 0, x), FIRST[in_unit(L, 0, x)])

                def down(g, i):
                    pe.wait_ge(hid_lo, at(NJ * L + 2 * g + 2, i, 4))
                    for x in range(2):
                        u = down_unit(L, g, x)
                        down_proj(u, FIRST[u], g % 2, i)

                with pe.Fori(0, (NG - 1) // 2) as i:
                    for g in (1, 2):
                        for x in range(4):
                            u = in_unit(L, g, x)
                            in_proj(u, FIRST[u], i)
                        down(g - 1, i)
                down(NG - 1, None)

            ffn(0)

            column_means(NAMED["stats2"], (sum_ok, SQ0[2] + KD), acc)
            pe.wait_ge(x_lo, 4 * KD)
            r0 = FIRST[U_QKV]
            with pe.Fori(0, NPAIR) as p:
                def opened(r):
                    pe.wait_ge(free, p * 20 + (r - 1))

                for x in range(3):
                    in_proj(U_QKV + x, r0 + x, p, 3, 20)

                pe.wait_ge(q_ok, p + 1)
                pe.wait_ge(o_free, p * 2 + 1)

                def score_sample(b):
                    pe.wait_ge(kv_in[b % 4], p * 64 + 16 * (b // 4 + 1))
                    for bank, lo, hi_ in ((0, 0, 512), (1, 512, NKEY)):
                        mm = nc.tensor.matmul(ob[0:64, bank, 0:hi_ - lo], qb[:, 64 * b:64 * b + 64],
                                              kvr[:, b % 4, lo:hi_], start=(b == 0), stop=(b == NB - 1))
                    mm.then_inc(kv_used, 1)

                def scores(n):
                    hh, b = BLOCKS[n]
                    opened(r0 + 4 + n)
                    out = reg[(r0 + 4 + n) % 2]
                    for lo in range(0, P * (b + 1), 512):
                        w = min(512, P * (b + 1) - lo)
                        mm = nc.tensor.matmul(out[:, lo // 512, 0:w], QT[HD * hh:HD * hh + HD, b * P:(b + 1) * P],
                                              KT[HD * hh:HD * hh + HD, lo:lo + w], start=True, stop=True)
                    mm.then_inc(full, 1)

                for b in range(4):
                    score_sample(b)
                pe.wait_ge(free, p * 20 + (r0 + 3))
                vr = reg[(r0 + 3) % 2]
                for t in range(8):
                    nc.tensor.transpose(vr[:, t // 4, (t % 4) * P:(t % 4 + 1) * P], VT[:, t * P:(t + 1) * P], ident[:, :])
                nc.tensor.transpose(vr[0:NS, 2, 0:P], VT[:, NP_:T], ident[:, :]).then_inc(full, 1)
                score_sample(4)
                score_sample(5)
                scores(0)
                scores(1)
                score_sample(6)
                score_sample(7)
                nc.tensor.matmul(ob[0:64, 1, NKEY - 512:NKEYS - 512], qa[:, :], KT[:, NP_:T],
                                 start=True, stop=True).then_inc(ss_full, 1)
                scores(2)

                def turn(n):
                    b = BLOCKS[n][1]
                    pe.wait_ge(p_ok, p * 16 + (n + 1))
                    for kb in range(b + 1):
                        mm = nc.tensor.transpose(reg[kb // 4][:, 2, (kb % 4) * P:(kb % 4 + 1) * P],
                                                 neg_s[:, n % 3, kb * P:(kb + 1) * P], ident[:, :])
                    mm.then_inc(pt_full, 1)

                def weigh(n):
                    hh, b = BLOCKS[n]
                    pe.wait_ge(pt_a, p * 16 + (n + 1))
                    if b >= 4:
                        pe.wait_ge(pt_b, p * 8 + (sum(x[1] >= 4 for x in BLOCKS[:n]) + 1))
                    if n == 0:
                        pe.wait_ge(ss_free, p + 1)
                    if n == 1:
                        pe.wait_ge(spt_ok, p * 2 + 2)
                    rows = slice(HD * hh, HD * hh + HD)
                    for kb in range(b + 1):
                        mm = nc.tensor.matmul(ob[rows, b // 4, (b % 4) * P:(b % 4 + 1) * P],
                                              vrow[:, kb, rows], pT[:, kb, :],
                                              start=(kb == 0), stop=(kb == b))
                    mm.then_inc(pv_ok, 1)

                def turn_sample():
                    pe.wait_ge(sp_ok, p + 1)
                    for t in range(KT_TILES):
                        nc.tensor.matmul(ob[:, 0, 64 * t:64 * t + 64], sps[:, t * P:(t + 1) * P], ident[0:64, 0:64],
                                         start=True, stop=True)
                    nc.tensor.matmul(ob[0:NS, 0, 448:512], sps[:, NKEY:NKEYS], ident[0:64, 0:64],
                                     start=True, stop=True).then_inc(spt_full, 1)

                def weigh_sample(b):
                    pe.wait_ge(kv_in[b % 4], p * 64 + 16 * (2 + b // 4 + 1))
                    out = reg[1][32 * (b % 4):32 * (b % 4) + 32, 2, 256 + P * (b // 4):256 + P * (b // 4) + P]
                    for t in range(KT_TILES):
                        nc.tensor.matmul(out, spT[:, t, 8 * b:8 * b + 32], kvr[:, b % 4, t * P:(t + 1) * P],
                                         start=(t == 0), stop=False)
                    nc.tensor.matmul(out, spT[0:NS, 7, 8 * b:8 * b + 32], vnew[:, :],
                                     start=False, stop=True).then_inc(kv_used, 1)

                for n in range(16):
                    turn(n)
                    if n + 3 < 16:
                        scores(n + 3)
                    for b in SAMPLE_STEPS.get(n, ()):
                        weigh_sample(b)
                    if n == 15:
                        pe.wait_ge(so_ok, p + 1)
                        for x in range(2):
                            mm = nc.tensor.transpose(reg[1][:, 2, 256 + P * x:256 + P * x + P], so[:, x, :], ident[:, :])
                        mm.then_inc(so_full, 1)
                    weigh(n)
                    if n == 0:
                        turn_sample()
                pe.wait_ge(so_free, p + 2)

            for m in range(KD):
                in_proj(U_WO + m, FIRST[U_WO + m], x_at=4 * KD if m == 0 else None)
            ffn(1)
            column_means(NAMED["stats4"], (sum_ok, SQ0[4] + KD), acc)

        @block.scalar
        def _(act):
            chain = Chain(act, a_chain)

            def square(s, m, src):
                k = SQ0[s] + m
                if k >= 2:
                    act.wait_ge(sum_ok, k - 1)
                nc.scalar.activation(sqb[k % 2], src, ACT.Square).then_inc(sq_ok, 1)

            def gain_hi(s, e, m):
                nc.scalar.activation(xs[:, 0, m, :], h[:, m, :], ACT.Copy, scale=pc("g", s * KD + m)).then_inc(x_hi, 1)

            def std(r, dst, scale, e):
                act.wait_ge(full, r + 1)
                nc.scalar.activation(tok(dst), region(r), ACT.Sqrt, bias=eps[:, e:e + 1], scale=scale).then_inc(std_ok, 1)

            def std_parts(n):
                act.wait_ge(st_full, n - 1)
                nc.scalar.activation(rst[:, 0:NP_].rearrange("p (x t) -> p x t", x=2), ob[:, :, :], ACT.Sqrt,
                                     bias=eps[:, 0:1]).then_inc(std_ok, 1)
                act.wait_ge(st_full, n)
                nc.scalar.activation(rst[:, NP_:], ob[:, 0, 0:NS], ACT.Sqrt, bias=eps[:, 0:1]).then_inc(std_ok, 1)

            act.wait_ge(par_in, 16)
            act.wait_ge(pads_ok, 1)
            split_hi(act, 0)
            for m in range(KD):
                h_ready(act, 0, m)
                gain_hi(0, 0, m)
                square(0, m, h[:, m, :])
                if m in (1, 3):
                    split_hi(act, (m + 1) // 2)
            hi_after(act, 0)
            std_parts(2)
            for c in range(CA):
                if c > 0:
                    hi_after(act, 2 * c)
                act.wait_ge(free, FIRST[2 * c] + 1)
                if c > 0:
                    act.wait_ge(glu_ok, c)
                nc.scalar.activation(sil[:, PAD:], tmp[:, :], ACT.Sigmoid).then_inc(sig_ok, 1)
                hi_after(act, 2 * c + 1)
            for u in range(8, 20):
                hi_after(act, u)
            act.wait_ge(full, LAST[19] + 1)
            for c in range(CA):
                act.wait_ge(free, FIRST[10 + 3 * c] + 1)
                nc.scalar.activation(xs[:, 0, CA + c, :], cb[:, c, :], ACT.Copy).then_inc(x_hi, 1)
            for c in range(CA):
                if c < CA - 1:
                    act.wait_ge(ycen_ok, c + 1)
                else:
                    act.wait_ge(free, NAMED["ln_mean"] + 1)
                square("ln", c, Y[c])
            std(NAMED["ln_var"], tmp[:, :], 2.0, 1)
            for c in range(CA):
                act.wait_ge(yn_ok, c + 1)
                chain(nc.scalar.activation(Y[c], Y[c], ACT.Silu, scale=pc("lg", c), bias=pc("lb", c)))
                nc.scalar.activation(xs[:, 0, c, :], Y[c], ACT.Copy).then_inc(x_hi, 1)
            for m in range(KD):
                hi_after(act, U_OUT + m)
                h_ready(act, 1, m)
                square(1, m, h[:, m, :])

            def ffn(L):
                s, e = (1, 2) if L == 0 else (3, 5)
                act.wait_ge(full, LAST[(U_OUT, U_WO)[L] + KD - 1] + 1)
                for m in range(KD):
                    h_ready(act, s, m)
                    gain_hi(s, e, m)
                hi_after(act, in_unit(L, 0, 0))
                std_parts((4, 6)[L])

                def chunk(g, c, i, skip=False):
                    A = At(i)
                    j = NJ * L + 2 * g + c
                    ug, uu = in_unit(L, g, 2 * c), in_unit(L, g, 2 * c + 1)
                    if not skip:
                        hi_after(act, ug, i)
                    act.wait_ge(conv_ok, A.chunk(j + 1))
                    nc.scalar.activation(sil[:, PAD:], acc[:, :], ACT.Silu).then_inc(silu_ok, 1)
                    hi_after(act, uu, i)
                    act.wait_ge(free, A.use(FIRST[uu] + 1))
                    nc.scalar.activation(hid[:, g % 2, c, 0, :], tmp[:, :], ACT.Copy).then_inc(hid_hi, 1)

                chunk(0, 0, None, skip=True)
                chunk(0, 1, None)
                with act.Fori(0, (NG - 1) // 2) as i:
                    for g in (1, 2):
                        for c in range(2):
                            chunk(g, c, i)
                        for x in range(2):
                            hi_after(act, down_unit(L, g - 1, x), i)
                s2 = 2 if L == 0 else 4
                for m in range(KD):
                    h_ready(act, s2, m)
                    if m == 0:
                        act.wait_ge(hid_lo, NJ * (L + 1))
                    square(s2, m, h[:, m, :])
                    if L == 0:
                        gain_hi(2, 3, m)
                    if m % 4 == 3:
                        hi_after(act, down_unit(L, NG - 1, m // 4))

            ffn(0)
            std(NAMED["stats2"], rst[:, :], 1.0, 0)
            r0 = FIRST[U_QKV]
            with act.Fori(0, NPAIR) as p:
                def probs(n):
                    b = BLOCKS[n][1]
                    act.wait_ge(free, p * 20 + (r0 + 5 + n))
                    nc.scalar.activation(neg_s[:, n % 3, 0:P * (b + 1)], neg_s[:, n % 3, 0:P * (b + 1)], ACT.Exp,
                                         bias=nmx[:, n:n + 1], scale=-1.0,
                                         accum_out=lsum[:, 0, n:n + 1]).then_inc(exp_ok, 1)

                def outputs(half):
                    act.wait_ge(pv_ok, p * 16 + (max(n for n in range(16) if BLOCKS[n][1] // 4 == half) + 1))
                    dst = att[:, ds(p, 1), 512 * half:512 * half + 512].rearrange("p a t -> p (a t)")
                    nc.scalar.activation(dst, ob[:, half, :], ACT.Copy).then_inc(o_free, 1)

                probs(0)
                probs(1)
                act.wait_ge(ss_free, p + 1)
                nc.scalar.activation(sps[:, :], sps[:, :], ACT.Exp, bias=snm[:, 0:1], scale=-1.0,
                                     accum_out=snm[:, 1:2]).then_inc(sp_exp, 1)
                for n in range(16):
                    b = BLOCKS[n][1]
                    if b >= 4:
                        act.wait_ge(pt_full, p * 16 + (n + 1))
                        nc.scalar.activation(pT[:, 4:b + 1, :], reg[1][:, 2, 0:P * (b - 3)].rearrange("p (k q) -> p k q", q=P),
                                             ACT.Copy).then_inc(pt_b, 1)
                    if n + 2 < 16:
                        probs(n + 2)
                    if n == 0:
                        act.wait_ge(spt_full, p + 1)
                        nc.scalar.activation(spT[:, 0:7, 0:64], ob[:, 0, 0:448].rearrange("p (t r) -> p t r", r=64),
                                             ACT.Copy).then_inc(spt_ok, 1)
                        nc.scalar.activation(spT[0:NS, 7, 0:64], ob[0:NS, 0, 448:512], ACT.Copy).then_inc(spt_ok, 1)
                    if n in (3, 5, 7):
                        x = (n - 3) // 2
                        split_hi(act, U_QKV + 3 + x, p, 3, p * 20 + (r0 + x + 1))
                    if n == 14:
                        act.wait_ge(kv_used, p * 16 + 16)
                        nc.scalar.activation(so[:, :, :], reg[1][:, 2, 256:512].rearrange("p (x c) -> p x c", c=P),
                                             ACT.Copy).then_inc(so_ok, 1)
                        outputs(1)
                outputs(0)
            act.wait_ge(so_free, NPAIR + 1)
            act.wait_ge(o_free, 1 + 2 * NPAIR)
            for m in range(KD):
                nc.scalar.activation(xs[:, 0, m, :], att[:, m, :], ACT.Copy).then_inc(x_hi, 1)
            for m in range(KD):
                hi_after(act, U_WO + m)
                h_ready(act, 3, m)
                square(3, m, h[:, m, :])
            ffn(1)
            std(NAMED["stats4"], rst[:, :], 1.0, 0)

        @block.gpsimd
        def _(pool):
            def add_square(s, m):
                k = SQ0[s] + m
                if m == 0:
                    return
                pool.wait_ge(sq_ok, k + 1)
                if m == 1:
                    if s == "ln":
                        pool.wait_ge(ycen_ok, 1)
                    if k > 1:
                        pool.wait_ge(sum_ok, k - 1)
                    nc.gpsimd.tensor_tensor(acc[:, :], sqb[(k - 1) % 2], sqb[k % 2], ALU.add).then_inc(sum_ok, 2)
                else:
                    pool.wait_ge(sum_ok, k)
                    nc.gpsimd.tensor_tensor(acc[:, :], acc[:, :], sqb[k % 2], ALU.add).then_inc(sum_ok, 1)

            split_lo(pool, 0)
            for m in range(KD):
                add_square(0, m)
                if m in (1, 3):
                    split_lo(pool, (m + 1) // 2)
            for u, (kind, c) in enumerate(MIX_ORDER):
                lo_after(pool, u)
                if kind == "s":
                    pool.wait_ge(sig_ok, c + 1)
                    nc.gpsimd.tensor_tensor(sil[:, PAD:], sil[:, PAD:], rst[:, :], ALU.mult).then_inc(sigr_ok, 1)
                elif kind == "C":
                    pool.wait_ge(free, FIRST[u] + 1)
                    nc.gpsimd.tensor_tensor(tmp[:, :], tmp[:, :], rst[:, :], ALU.mult).then_inc(cr_ok, 1)
                elif kind == "X":
                    pool.wait_ge(cb_ok, c + 1)
                    nc.gpsimd.tensor_tensor(cb[:, c, :], cb[:, c, :], rst[:, :], ALU.mult).then_inc(cbr_ok, 1)
            for c in range(CA):
                add_square("ln", c)
            for m in range(KD):
                lo_after(pool, U_OUT + m)
                add_square(1, m)

            def ffn(L):
                def chunk(g, c, i):
                    A = At(i)
                    jj = 2 * g + c
                    j = NJ * L + jj
                    ug, uu = in_unit(L, g, 2 * c), in_unit(L, g, 2 * c + 1)
                    lo_after(pool, ug, i)
                    pool.wait_ge(free, A.use(FIRST[ug] + 1))
                    if g == 0 and c == 0:
                        pool.wait_ge(sx_in, 16 * NB * (L + 1))
                        if L == 1:
                            pool.wait_ge(ff_out, 16 * (1 + NB))
                    if i is None:
                        sx_j, pf_j = sx[:, jj, :, KF - 1:], pf_st[:, jj, :]
                    else:
                        sx_j = sx[:, ds(i * 4 + jj, 1), :, KF - 1:].rearrange("p a b q -> p (a b) q")
                        pf_j = pf_st[:, ds(i * 4 + jj, 1), :].rearrange("p a k -> p (a k)")
                    nc.gpsimd.tensor_copy(sx_j, gbuf[:, PAD + NP_:].rearrange("p (b q) -> p b q", b=NB)).then_inc(hist_ok, 1)
                    nc.gpsimd.tensor_copy(pf_j, gbuf[:, PAD + NP_ - KF + 1:PAD + NP_]).then_inc(hist_ok, 1)
                    pool.wait_ge(silu_ok, A.chunk(j + 1))
                    nc.gpsimd.tensor_tensor(sil[:, PAD:], sil[:, PAD:], rst[:, :], ALU.mult).then_inc(silr_ok, 1)
                    lo_after(pool, uu, i)

                for c in range(2):
                    chunk(0, c, None)
                with pool.Fori(0, (NG - 1) // 2) as i:
                    for g in (1, 2):
                        for c in range(2):
                            chunk(g, c, i)
                        for x in range(2):
                            lo_after(pool, down_unit(L, g - 1, x), i)
                s2 = 2 if L == 0 else 4
                for m in range(KD):
                    add_square(s2, m)
                    if m % 4 == 3:
                        lo_after(pool, down_unit(L, NG - 1, m // 4))

            ffn(0)
            with pool.Fori(0, NPAIR) as p:
                for x in range(3):
                    split_lo(pool, U_QKV + 3 + x, p, 3)
            for m in range(KD):
                lo_after(pool, U_WO + m)
                add_square(3, m)
            ffn(1)

        @block.vector
        def _(dve):
            chain = Chain(dve, v_chain)

            def opened(r, i=None, step=24):
                dve.wait_ge(full, at(r + 1, i, step))
                if i is not None or r >= 1:
                    dve.wait_ge(free, at(r, i, step))

            def emptied(r, i=None, step=24):
                dve.wait_ge(free, at(r + 1, i, step))

            def factor(r, dst, n):
                opened(r)
                dve.wait_ge(std_ok, n)
                nc.vector.reciprocal(dst, dst).then_inc(free, 1)
                emptied(r)

            def factor_parts(n):
                dve.wait_ge(std_ok, n - 1)
                chain(nc.vector.reciprocal(rst[:, 0:NP_], rst[:, 0:NP_]))
                dve.wait_ge(std_ok, n)
                chain(nc.vector.reciprocal(rst[:, NP_:], rst[:, NP_:]))

            def gain_lo(s, e, m):
                k = e * KD + m
                dve.wait_ge(x_hi, k + 1)
                nc.vector.scalar_tensor_tensor(out=xs[:, 1, m, :], in0=h[:, m, :], scalar=pc("g", s * KD + m),
                                               in1=xs[:, 0, m, :].bitcast(F32), op0=ALU.mult,
                                               op1=ALU.subtract).then_inc(x_lo, 1)

            def rest_lo(e, n, m, src):
                dve.wait_ge(x_hi, e * KD + n + 1)
                nc.vector.tensor_tensor(xs[:, 1, m, :], src, xs[:, 0, m, :].bitcast(F32), ALU.subtract).then_inc(x_lo, 1)

            def add_to_h(r, m, i=None):
                opened(r, i)
                nc.vector.tensor_tensor(tok(h[:, m, :]), region(r), tok(h[:, m, :]), ALU.add).then_inc(free, 1)

            for b in (g0, g1, g2, g3, sil):
                chain(nc.vector.memset(b[:, 0:PAD], 0.0))
            chain(nc.vector.memset(eps[:, 0:1], RMS_EPS))
            nc.vector.memset(eps[:, 1:2], LN_EPS).then_inc(pads_ok, 1)
            dve.wait_ge(pads_ok, 1)
            dve.wait_ge(par_in, 16)
            for m in range(KD):
                gain_lo(0, 0, m)

            def conv_tap(c, k):
                w = pc("wa", c * KA + k)
                y, src = Y[c][:, 0:NP_], G[c][:, k:k + NP_]
                if k == 0:
                    conv_sample(c)
                    chain(nc.vector.tensor_scalar(y, src, w, pc("ba", c), ALU.mult, ALU.add))
                else:
                    chain(nc.vector.scalar_tensor_tensor(out=y, in0=src, scalar=w, in1=y, op0=ALU.mult, op1=ALU.add))

            def conv_sample(c):
                w0 = cols["wa"] + c * KA
                w = pt[:, w0:w0 + KA].unsqueeze(1).to_broadcast([P, NB, KA])
                ys = Y[c][:, NP_:].rearrange("p (b q) -> p b q", b=NB)
                for q in range(NQ):
                    chain(nc.vector.tensor_tensor(prod[:, q % 2, :, :], AS[:, c, :, q:q + KA], w, ALU.mult))
                    chain(nc.vector.tensor_reduce(ys[:, :, q], prod[:, q % 2, :, :], mybir.AxisListType.X, ALU.add))
                chain(nc.vector.tensor_scalar(Y[c][:, NP_:], Y[c][:, NP_:], pc("ba", c), None, ALU.add))

            def mixer_step(kind, c, r):
                opened(r)
                if kind == "s":
                    if c > 0:
                        dve.wait_ge(sig_ok, c)
                    nc.vector.tensor_tensor(tok(tmp[:, :]), region(r), tok(rst[:, :]), ALU.mult).then_inc(free, 1)
                elif kind == "a":
                    g = G[c][:, PAD:]
                    dve.wait_ge(sigr_ok, c + 1)
                    nc.vector.tensor_tensor(tok(g), region(r), tok(sil[:, PAD:]), ALU.mult).then_inc(free, 1)
                    emptied(r)
                    dve.wait_ge(st_in, 16 * 2 * CA)
                    chain(nc.vector.tensor_copy(AS[:, c, :, PAD:], g[:, NP_:].rearrange("p (b q) -> p b q", b=NB)))
                    nc.vector.tensor_copy(pa_st[:, c, :], G[c][:, NP_:NP_ + PAD]).then_inc(glu_ok, 1)
                    dve.wait_ge(glu_ok, c + 1)
                elif kind == "C":
                    nc.vector.tensor_tensor(tok(tmp[:, :]), region(r), tok(rst[:, :]), ALU.mult).then_inc(free, 1)
                elif kind == "X":
                    b = sil[:, PAD:]
                    dve.wait_ge(cr_ok, c + 1)
                    nc.vector.tensor_tensor(tok(b), region(r), tok(tmp[:, :]), ALU.mult).then_inc(free, 1)
                    emptied(r)
                    chain(nc.vector.tensor_copy(BS[:, c, :, KB - 1:], b[:, NP_:].rearrange("p (b q) -> p b q", b=NB)))
                    chain(nc.vector.tensor_copy(pb_st[:, c, :], b[:, NP_ - KB + 1:NP_]))
                    for k in range(KB):
                        w = pc("wb", c * KB + k)
                        src = sil[:, PAD - KB + 1 + k:PAD - KB + 1 + k + NP_]
                        new = BS[:, c, :, k:k + NQ]
                        y, ys = cb[:, c, 0:NP_], cb[:, c, NP_:].rearrange("p (b q) -> p b q", b=NB)
                        if k == 0:
                            chain(nc.vector.tensor_scalar(y, src, w, None, ALU.mult))
                            chain(nc.vector.tensor_scalar(ys, new, w, None, ALU.mult))
                        else:
                            chain(nc.vector.scalar_tensor_tensor(out=y, in0=src, scalar=w, in1=y, op0=ALU.mult, op1=ALU.add))
                            ins = nc.vector.scalar_tensor_tensor(out=ys, in0=new, scalar=w, in1=ys, op0=ALU.mult, op1=ALU.add)
                            if k < KB - 1:
                                chain(ins)
                            else:
                                ins.then_inc(cb_ok, 1)
                else:
                    dve.wait_ge(cbr_ok, c + 1)
                    nc.vector.tensor_tensor(tok(cb[:, c, :]), region(r), tok(cb[:, c, :]), ALU.mult).then_inc(free, 1)
                    emptied(r)

            factor_parts(2)
            taps = [(c, k) for c in range(CA) for k in range(KA)]
            PER = 7
            for u, (kind, c) in enumerate(MIX_ORDER):
                mixer_step(kind, c, FIRST[u])
                if u >= 1:
                    for tc, tk in taps[PER * (u - 1):PER * u]:
                        conv_tap(tc, tk)
            for tc, tk in taps[PER * 19:]:
                conv_tap(tc, tk)


            chain(nc.vector.tensor_tensor(acc[:, :], Y[0], Y[1], ALU.add))
            chain(nc.vector.tensor_tensor(acc[:, :], acc[:, :], Y[2], ALU.add))
            nc.vector.tensor_tensor(acc[:, :], acc[:, :], Y[3], ALU.add).then_inc(ysum_ok, 1)
            for c in range(CA):
                rest_lo(1, c, CA + c, cb[:, c, :])
            r = NAMED["ln_mean"]
            opened(r)
            for c in range(CA):
                if c == CA - 1:
                    dve.wait_ge(ycen_ok, c)
                ins = nc.vector.scalar_tensor_tensor(out=tok(Y[c]), in0=region(r), scalar=-2.0, in1=tok(Y[c]),
                                                     op0=ALU.mult, op1=ALU.add)
                ins.then_inc(ycen_ok if c < CA - 1 else free, 1)
            factor(NAMED["ln_var"], tmp[:, :], 3)
            for c in range(CA):
                nc.vector.tensor_tensor(Y[c], Y[c], tmp[:, :], ALU.mult).then_inc(yn_ok, 1)
            for c in range(CA):
                rest_lo(1, CA + c, c, Y[c])
            for m in range(KD):
                add_to_h(FIRST[U_OUT + m], m)

            def ffn(L):
                s, e = (1, 2) if L == 0 else (3, 5)
                for m in range(KD):
                    gain_lo(s, e, m)
                factor_parts((5, 8)[L])

                def hidden_lo(g, c, i):
                    A = At(i)
                    dve.wait_ge(hid_hi, A.chunk(NJ * L + 2 * g + c + 1))
                    nc.vector.tensor_tensor(hid[:, g % 2, c, 1, :], tmp[:, :], hid[:, g % 2, c, 0, :].bitcast(F32),
                                            ALU.subtract).then_inc(hid_lo, 1)

                def chunk(g, c, i):
                    A = At(i)
                    jj = 2 * g + c
                    j = NJ * L + jj
                    rg, ru = FIRST[in_unit(L, g, 2 * c)], FIRST[in_unit(L, g, 2 * c + 1)]
                    opened(rg, i)
                    if j > 0:
                        dve.wait_ge(hist_ok, at(2 * j, i, 8))
                    nc.vector.tensor_tensor(tok(gbuf[:, PAD:]), region(rg), tok(rst[:, :]), ALU.mult).then_inc(free, 1)
                    if c == 1:
                        hidden_lo(g, 0, i)
                    emptied(rg, i)
                    if j > 0:
                        dve.wait_ge(silu_ok, A.chunk(j))
                    dj = jj if i is None else i * 4 + jj
                    for k in (KF - 1, 1, 0):
                        w = pc_dyn("wf", dj * KF + (L * NJ * KF + k))
                        src, y = gbuf[:, PAD - KF + 1 + k:PAD - KF + 1 + k + NP_], acc[:, 0:NP_]
                        if k == KF - 1:
                            chain(nc.vector.tensor_scalar(y, src, w, None, ALU.mult))
                        else:
                            chain(nc.vector.scalar_tensor_tensor(out=y, in0=src, scalar=w, in1=y, op0=ALU.mult, op1=ALU.add))
                    dve.wait_ge(hist_ok, at(2 * j + 2, i, 8))
                    y = acc[:, NP_:].rearrange("p (b q) -> p b q", b=NB)
                    for k in (KF - 1, 1, 0):
                        w = pc_dyn("wf", dj * KF + (L * NJ * KF + k))
                        if i is None:
                            src = sx[:, jj, :, k:k + NQ]
                        else:
                            src = sx[:, ds(i * 4 + jj, 1), :, k:k + NQ].rearrange("p a b q -> p (a b) q")
                        if k == KF - 1:
                            chain(nc.vector.tensor_scalar(y, src, w, None, ALU.mult))
                        else:
                            ins = nc.vector.scalar_tensor_tensor(out=y, in0=src, scalar=w, in1=y, op0=ALU.mult, op1=ALU.add)
                            if k:
                                chain(ins)
                            else:
                                ins.then_inc(conv_ok, 1)
                    opened(ru, i)
                    dve.wait_ge(silr_ok, A.chunk(j + 1))
                    if j > 0:
                        dve.wait_ge(hid_lo, A.chunk(j))
                    nc.vector.tensor_tensor(tok(tmp[:, :]), region(ru), tok(sil[:, PAD:]), ALU.mult).then_inc(free, 1)

                def group(g, i):
                    for c in range(2):
                        chunk(g, c, i)
                    if g == 0:
                        hidden_lo(0, 1, i)
                        return
                    for x in range(2):
                        u = down_unit(L, g - 1, x)
                        for m in range(4):
                            add_to_h(FIRST[u] + m, 4 * x + m, i)
                            if x == 0 and m == 0:
                                hidden_lo(g, 1, i)

                group(0, None)
                with dve.Fori(0, (NG - 1) // 2) as i:
                    chain.restart()
                    for g in (1, 2):
                        group(g, i)
                for m in range(KD):
                    add_to_h(FIRST[down_unit(L, NG - 1, m // 4)] + m % 4, m)
                    if L == 0 and m > 0:
                        dve.wait_ge(free, FIRST[down_unit(L, NG - 1, (m - 1) // 4)] + (m - 1) % 4 + 1)
                        gain_lo(2, 3, m - 1)

            ffn(0)
            gain_lo(2, 3, KD - 1)
            factor(NAMED["stats2"], rst[:, :], 6)
            dve.wait_ge(st_out, 16 * (2 + 2 * CA))
            dve.wait_ge(ff_out, 16 * (1 + NB))
            chain(nc.vector.memset(qb[:, :], 0.0))
            nc.vector.memset(qa[:, :], 0.0).then_inc(so_free, 1)
            dve.wait_ge(so_free, 1)
            nc.vector.memset(spT[:, :, :], 0.0).then_inc(o_free, 1)
            dve.wait_ge(o_free, 1)
            dve.wait_ge(kv_out, 16)
            dve.wait_ge(x_lo, 4 * KD)
            dve.wait_ge(x_hi, 4 * KD)
            r0 = FIRST[U_QKV]
            with dve.Fori(0, NPAIR) as p:
                chain.restart()

                def wait(s, step, base):
                    dve.wait_ge(s, (p if step == 1 else p * step) + base)

                def settle():
                    chain(nc.vector.tensor_copy(eps[0:1, 2:3], eps[0:1, 0:1]))

                opened(r0, p, 20)
                nc.vector.scalar_tensor_tensor(out=tok(QT[:, :]), in0=region(r0), scalar=HD ** -0.5, in1=tok(rst[:, :]),
                                               op0=ALU.mult, op1=ALU.mult).then_inc(free, 1)
                emptied(r0, p, 20)
                for hh in range(2):
                    rows = slice(HD * hh, HD * hh + HD)
                    src = QT[rows, NP_:].rearrange("p (b q) -> p b q", b=NB)
                    qb_v = qb[rows, :].rearrange("p (b s) -> p b s", s=72)[:, :, NQ * hh:NQ * hh + NQ]
                    qa_v = qa[rows, :].rearrange("p (b s) -> p b s", s=8)[:, :, NQ * hh:NQ * hh + NQ]
                    chain(nc.vector.tensor_copy(qb_v, src))
                    ins = nc.vector.tensor_copy(qa_v, src)
                    if hh == 0:
                        chain(ins)
                    else:
                        ins.then_inc(q_ok, 1)
                opened(r0 + 1, p, 20)
                wait(kv_out, 32, 16)
                nc.vector.tensor_tensor(tok(KT[:, :]), region(r0 + 1), tok(rst[:, :]), ALU.mult).then_inc(free, 1)
                opened(r0 + 2, p, 20)
                nc.vector.tensor_tensor(tok(VT[:, :]), region(r0 + 2), tok(rst[:, :]), ALU.mult).then_inc(free, 1)

                opened(r0 + 3, p, 20)
                vr = reg[(r0 + 3) % 2]
                chain(nc.vector.tensor_copy(vrow[:, :, :], vr[:, 0:2, :].rearrange("p a (t c) -> p (a t) c", c=P)))
                nc.vector.tensor_copy(vnew[:, :], vr[0:NS, 2, 0:P]).then_inc(free, 1)

                def neg_scores(n):
                    hh, b = BLOCKS[n]
                    r = r0 + 4 + n
                    opened(r, p, 20)
                    if n in (0, 2):
                        wait(wt_in[hh], 16, 16)
                    w = P * (b + 1)
                    settle()
                    nc.vector.tensor_tensor_reduce(out=neg_s[:, n % 3, 0:w],
                                                   in0=reg[r % 2][:, 0:2, :].rearrange("p a c -> p (a c)")[:, 0:w],
                                                   in1=wt[:, hh, 1024 - w:1024], scale=-1.0, scalar=3.0e38,
                                                   op0=ALU.add, op1=ALU.min, accum_out=nmx[:, n:n + 1]).then_inc(free, 1)

                def norm(n):
                    w = P * (BLOCKS[n][1] + 1)
                    wait(exp_ok, 16, n + 1)
                    chain(nc.vector.reciprocal(lsum[:, 1, n:n + 1], lsum[:, 0, n:n + 1]))
                    nc.vector.tensor_scalar(neg_s[:, n % 3, 0:w], neg_s[:, n % 3, 0:w], lsum[:, 1, n:n + 1], None,
                                            ALU.mult).then_inc(p_ok, 1)

                neg_scores(0)
                neg_scores(1)
                norm(0)
                wait(ss_full, 1, 1)
                wait(sb_in, 16, 16)
                settle()
                nc.vector.tensor_tensor_reduce(out=sps[:, :], in0=ob[0:64, :, :].rearrange("p a c -> p (a c)")[:, 0:NKEYS],
                                               in1=sps[:, :], scale=-1.0, scalar=3.0e38, op0=ALU.add, op1=ALU.min,
                                               accum_out=snm[:, 0:1]).then_inc(ss_free, 1)
                for n in range(16):
                    b = BLOCKS[n][1]
                    wait(pt_full, 16, n + 1)
                    k = min(b + 1, 4)
                    nc.vector.tensor_copy(pT[:, 0:k, :], reg[0][:, 2, 0:P * k].rearrange("p (k q) -> p k q", q=P)).then_inc(pt_a, 1)
                    if n + 2 < 16:
                        neg_scores(n + 2)
                    if n + 1 < 16:
                        norm(n + 1)
                    if n == 0:
                        wait(sp_exp, 1, 1)
                        chain(nc.vector.reciprocal(snm[:, 2:3], snm[:, 1:2]))
                        nc.vector.tensor_scalar(sps[:, :], sps[:, :], snm[:, 2:3], None, ALU.mult).then_inc(sp_ok, 1)
                    if n == 15:
                        wait(so_full, 1, 1)
                        for hh in range(2):
                            rows = slice(HD * hh, HD * hh + HD)
                            dst = att[rows, ds(p, 1), NP_:].rearrange("p a (b q) -> p (a b) q", b=NB)
                            src = reg[1][rows, 2, 256:512].rearrange("p (b r) -> p b r", b=NB)[:, :, NQ * hh:NQ * hh + NQ]
                            ins = nc.vector.tensor_copy(dst, src)
                            if hh == 0:
                                chain(ins)
                            else:
                                ins.then_inc(so_free, 1)
            dve.wait_ge(o_free, 1 + 2 * NPAIR)
            dve.wait_ge(so_free, NPAIR + 1)
            for m in range(KD):
                rest_lo(4, m, m, att[:, m, :])
            dve.wait_ge(kv_out, 16 + 32 * NPAIR)
            dve.wait_ge(h_back, 16)
            chain(nc.vector.memset(g3[:, 0:PAD], 0.0))
            for m in range(KD):
                add_to_h(FIRST[U_WO + m], m)
            ffn(1)
            factor(NAMED["stats4"], rst[:, :], 9)
            for m in range(KD):
                nc.vector.scalar_tensor_tensor(out=h[:, m, :], in0=h[:, m, :], scalar=pc("g", 4 * KD + m), in1=rst[:, :],
                                               op0=ALU.mult, op1=ALU.mult).then_inc(y_ok, 1)
    return nc


def branch_bias(dist, slope):
    count = sum((((dist >= 0) & (dist <= w) & (dist % d == 0)).astype(np.float32) for w, d in BRANCHES))
    return np.where(count > 0, -slope * dist.astype(np.float32) + np.log(np.maximum(count, 1)), MASKED).astype(np.float32)


def bias_tables():
    slopes = (2.0 ** (-8.0 * np.arange(1, NH + 1) / NH)).astype(np.float32)
    dist = np.arange(P)[:, None] + (NP_ - P) - np.arange(NP_)[None, :]
    prompt = np.zeros((NH + 2, P, NP_), np.float32)
    for hd in range(NH):
        prompt[hd] = branch_bias(dist, slopes[hd])
    pos = key_positions()
    sample = np.zeros((NPAIR + 1, NB, 2, NQ, NKEYS), np.float32)
    for hd in range(NH):
        for j in range(NQ):
            s = sample[hd // 2, :, hd % 2, j]
            s[:, :NKEY] = branch_bias(PAST + j - pos, slopes[hd])
            s[:, NKEY:] = MASKED
            for b in range(NB):
                s[b, NKEY + NQ * b:NKEY + NQ * (b + 1)] = branch_bias(j - np.arange(NQ), slopes[hd])
    return prompt, sample.reshape(NPAIR + 1, 2 * NS, NKEYS)


def key_positions():
    far = (16 * np.arange((PAST - 512) // 16)[:, None] + np.arange(NQ)[None, :]).ravel()
    return np.concatenate([far, np.arange(PAST - 512, PAST)])


def kernel(**inputs):
    import concourse.bacc as bacc
    from concourse.bass_utils import run_bass_kernel_spmd

    a = {k: np.asarray(v) for k, v in inputs.items()}

    def chunks(x):
        n = x.shape[-1] // P
        y = x.reshape(x.shape[:-1] + (n, P))
        return np.ascontiguousarray(np.moveaxis(np.moveaxis(y, -1, 0), -1, 1))

    xT = np.concatenate([chunks(a["x_prompt"][0]), chunks(a["x_sample"].reshape(NS, D))], axis=2)

    def col_unit(w, col):
        return w[:, col:col + P].reshape(KD, P, P).transpose(1, 0, 2).reshape(P, 1024)

    def row_unit(w, g, half):
        return w[2 * P * g:2 * P * (g + 1), 512 * half:512 * half + 512].reshape(2, P, 512).transpose(1, 0, 2).reshape(P, 1024)

    units = []
    starts = {"a": 0, "s": 512, "G": 1024, "C": 1536, "X": 2048}
    for kind, c in MIX_ORDER:
        units.append(col_unit(a["w_in_ab"][0], starts[kind] + P * c))
    for m in range(KD):
        units.append(col_unit(a["w_out_ab"][0], P * m))

    def ffn_units(L):
        w_in, w_dn, out = a["w_ffn_in"][L], a["w_down"][L], []
        for g in range(NG):
            for c in range(2):
                out += [col_unit(w_in, P * (2 * g + c)), col_unit(w_in, DFF + P * (2 * g + c))]
            if g > 0:
                out += [row_unit(w_dn, g - 1, x) for x in range(2)]
        return out + [row_unit(w_dn, NG - 1, x) for x in range(2)]

    units += ffn_units(0)
    for p in range(NPAIR):
        units += [col_unit(a["w_qkv"][0], x * D + P * p) for x in range(3)]
    for m in range(KD):
        units.append(col_unit(a["w_o"][0], P * m))
    units += ffn_units(1)
    wstream = np.stack(units + [np.zeros_like(units[0])])

    def flat(x):
        return x.reshape(P, -1)

    par = np.concatenate([
        flat(np.moveaxis(chunks(np.stack([a["g_mix"][0], a["g_ffn"][0], a["g_mix"][1], a["g_ffn"][1], a["g_final"]])), 2, 1)),
        flat(chunks(a["conv_a_w"][0])), flat(chunks(a["conv_a_b"][0])), flat(chunks(a["ln_a_g"][0])),
        flat(chunks(a["ln_a_b"][0])), flat(chunks(a["conv_b_w"][0])),
        flat(np.moveaxis(chunks(a["conv_f_w"]), 2, 1)),
    ], axis=1)

    pos = key_positions()
    kg = a["cache_k"][0][:, pos].reshape(NB, NKEY, NPAIR, P)
    vg = a["cache_v"][0][:, pos].reshape(NB, KT_TILES, P, NPAIR, P)
    kv = np.concatenate([kg.transpose(2, 0, 3, 1), vg.transpose(3, 0, 2, 1, 4).reshape(NPAIR, NB, P, NKEY)], axis=1)
    wtab, sbias = bias_tables()
    arrays = {
        "xT": xT, "wstream": wstream, "par": par, "ident": np.eye(P, dtype=np.float32),
        "ones": np.full((P, P), 1.0 / D, np.float32),
        "stA": chunks(a["state_conv_a"][0]), "stB": chunks(a["state_conv_b"][0]),
        "stF": np.ascontiguousarray(np.moveaxis(chunks(a["state_ffn"]), 2, 0)),
        "kv": kv, "wtab": wtab, "sbias": sbias,
        "cache_k": a["cache_k"][0].reshape(NB, PAST * D), "cache_v": a["cache_v"][0].reshape(NB, PAST * D),
    }
    outs = {
        "y": (P, KD, T), "pA": (P, CA, PAD), "sA": (P, CA, NB, PAD), "pB": (P, CA, KB - 1), "sB": (P, CA, NB, KB - 1),
        "kT": (NPAIR, P, T), "vT": (NPAIR, P, T), "sk": (NB, KEPT * D), "sv": (NB, KEPT * D),
        "pF": (2, P, NJ, KF - 1), "sF": (2, P, NJ, NB, KF - 1),
    }
    nc = bacc.Bacc("TRN2", target_bir_lowering=False, num_devices=1)
    arrays = {f"in_{k}": np.ascontiguousarray(v) for k, v in arrays.items()}
    ins = [nc.dram_tensor(k, v.shape, F32, kind="ExternalInput").ap() for k, v in arrays.items()]
    spill = nc.dram_tensor("h_spill", (P, KD, T), F32, kind="Internal").ap()
    res = [nc.dram_tensor(f"out_{k}", s, F32, kind="ExternalOutput").ap() for k, s in outs.items()]
    build(nc, *ins, spill, *res)
    r = run_bass_kernel_spmd(nc, [arrays], core_ids=[0]).results[0]
    o = {k: np.asarray(r[f"out_{k}"]) for k in outs}

    def rows(x):
        y = np.moveaxis(np.moveaxis(x, 1, -1), 0, -1)
        return y.reshape(y.shape[:-2] + (-1,))

    y = rows(o["y"])
    kT, vT = (o[k].transpose(2, 0, 1).reshape(T, D) for k in ("kT", "vT"))

    def cache(kept, new):
        return np.concatenate([kept.reshape(NB, KEPT, NH, HD), new.reshape(NB, NQ, NH, HD)], axis=1)[None]

    return (y[:NP_][None], y[NP_:].reshape(NB, NQ, D),
            rows(o["pA"])[None, None], rows(o["sA"])[None],
            rows(o["pB"])[None, None], rows(o["sB"])[None],
            kT[:NP_].reshape(1, 1, NP_, NH, HD), cache(o["sk"], kT[NP_:]),
            vT[:NP_].reshape(1, 1, NP_, NH, HD), cache(o["sv"], vT[NP_:]),
            np.stack([rows(x)[None] for x in o["pF"]]), np.stack([rows(x) for x in o["sF"]]))
```
